# Optimizing a Trainium2 kernel written in Bass

```python
import jax
import jax.numpy as jnp
from jax import lax
import numpy as np

D_MODEL = 1024
BATCH = 1
SEQ = 1024
DEPTH = 2

N_MIXERS = 2
N_FNET = (DEPTH + 1) // 2
N_RWKV = DEPTH // 2
FNET_GROUPS = 4
FNET_GROUP_DIM = D_MODEL // FNET_GROUPS
HEAD_DIM = 64
N_HEADS = D_MODEL // HEAD_DIM
N_DIR = 2
R_DECAY = max(32, int(round(1.8 * D_MODEL ** 0.5 / 32)) * 32)
R_AAA = max(32, int(round(1.8 * D_MODEL ** 0.5 / 32)) * 32)
R_GATE = max(32, int(round(0.6 * D_MODEL ** 0.8 / 32)) * 32)
D_FF = 256 * ((8 * D_MODEL // 3 + 255) // 256)
CONV_WIDTH = 3
RMS_EPS = 1e-6
GN_EPS = 64e-5
L2_EPS = 1e-12

kernel_name = 'hybrid_fnet_rwkv7_encoder'

def rms_norm(x, g):
    xf = x.astype(jnp.float32)
    y = xf * lax.rsqrt(jnp.mean(xf * xf, axis=-1, keepdims=True) + RMS_EPS)
    return (y * g.astype(jnp.float32)).astype(x.dtype)

def shift_prev(t):
    return jnp.pad(t, ((0, 0), (1, 0), (0, 0)))[:, :-1]

def shift_next(t):
    return jnp.pad(t, ((0, 0), (0, 1), (0, 0)))[:, 1:]

def fourier_mixer(h, w_o, b_o):
    b, s, d = h.shape
    hg = h.astype(jnp.float32).reshape(b, s, FNET_GROUPS, FNET_GROUP_DIM)
    f = jnp.fft.fftn(hg, axes=(1, 3), norm='ortho').real
    return f.reshape(b, s, d).astype(h.dtype) @ w_o + b_o

def wkv7_scan(r, w, k, v, a, bb):
    def step(state, inp):
        r_t, w_t, k_t, v_t, a_t, b_t = inp
        sa = jnp.einsum('zbhij,zbhj->zbhi', state, a_t)
        state = (state * w_t[..., None, :]
                 + sa[..., :, None] * b_t[..., None, :]
                 + v_t[..., :, None] * k_t[..., None, :])
        y_t = jnp.einsum('zbhij,zbhj->zbhi', state, r_t)
        return state, y_t
    _, dirs, bsz, nh, n = r.shape
    state0 = jnp.zeros((dirs, bsz, nh, n, n), jnp.float32)
    _, y = lax.scan(step, state0, (r, w, k, v, a, bb))
    return y

def rwkv7_mixer(h, mu, w_rkv, w0, w1, w2, a0, a1, a2, g1, g2, k_k, k_a, r_k, ln_w, ln_b, w_o):
    bsz, s, d = h.shape
    d_prev = shift_prev(h) - h
    d_next = shift_next(h) - h

    def mix(i):
        return h + d_prev * mu[0, i] + d_next * mu[1, i]

    f32 = lambda t: t.astype(jnp.float32)
    heads = lambda t: t.reshape(t.shape[:-1] + (N_HEADS, HEAD_DIM))
    r = f32(mix(0) @ w_rkv[0])
    k = f32(mix(1) @ w_rkv[1])
    v = f32(mix(2) @ w_rkv[2])
    xw, xa, xg = mix(3), mix(4), mix(5)
    lw = jnp.einsum('zbsr,zrd->zbsd', jnp.tanh(jnp.einsum('bsd,zdr->zbsr', xw, w1)), w2)
    w_log = -jax.nn.softplus(-(f32(w0)[:, None, None, :] + f32(lw))) - 0.5
    decay = jnp.exp(-jnp.exp(w_log))
    la = jnp.einsum('zbsr,zrd->zbsd', jnp.einsum('bsd,zdr->zbsr', xa, a1), a2)
    a_gate = jax.nn.sigmoid(f32(a0)[:, None, None, :] + f32(la))
    g = jax.nn.sigmoid(xg @ g1) @ g2
    kk = heads(k * f32(k_k))
    kk = kk / jnp.maximum(jnp.linalg.norm(kk, axis=-1, keepdims=True), L2_EPS)
    k_dir = heads(k[None] * (1.0 + (a_gate - 1.0) * f32(k_a)))
    b_dir = kk[None] * heads(a_gate)
    both = lambda t: jnp.stack([t, jnp.flip(t, axis=1)])
    orient = lambda t: jnp.stack([t[0], jnp.flip(t[1], axis=1)])
    tm = lambda t: jnp.moveaxis(t, 2, 0)
    y = wkv7_scan(tm(both(heads(r))), tm(orient(heads(decay))), tm(orient(k_dir)),
                  tm(both(heads(v))), tm(both(-kk)), tm(orient(b_dir)))
    y = jnp.moveaxis(y, 0, 2)
    y = y[0] + jnp.flip(y[1], axis=1)
    mean = jnp.mean(y, axis=-1, keepdims=True)
    var = jnp.mean(jnp.square(y - mean), axis=-1, keepdims=True)
    y = (y - mean) * lax.rsqrt(var + GN_EPS) * heads(f32(ln_w)) + heads(f32(ln_b))
    bonus = jnp.sum(heads(r) * (k_dir[0] + k_dir[1]) * f32(r_k), axis=-1, keepdims=True) * heads(v)
    out = (y + bonus).reshape(bsz, s, d).astype(h.dtype) * g
    return out @ w_o

def conv_ffn(h, w_in, conv_w, conv_b, w_out):
    u = h @ w_in
    u = shift_prev(u) * conv_w[0] + u * conv_w[1] + shift_next(u) * conv_w[2] + conv_b
    gate, val = jnp.split(u, 2, axis=-1)
    return (jax.nn.silu(gate) * val) @ w_out

def setup_inputs(seed: int = 0) -> dict:
    key = jax.random.key(seed)
    ks = iter(jax.random.split(key, 32))
    nrm = lambda shape, scale: jax.random.normal(next(ks), shape, jnp.float32) * scale
    uni = lambda shape, lo, hi: jax.random.uniform(next(ks), shape, jnp.float32, lo, hi)
    d = D_MODEL
    return {
        'x': nrm((BATCH, SEQ, d), 1.0),
        'norm_mix_g': 1.0 + nrm((DEPTH, d), 0.05),
        'norm_ffn_g': 1.0 + nrm((DEPTH, d), 0.05),
        'norm_final_g': 1.0 + nrm((d,), 0.05),
        'fnet_w_o': nrm((N_FNET, d, d), d ** -0.5),
        'fnet_b_o': nrm((N_FNET, d), 0.01),
        'rwkv_mu': uni((N_RWKV, 2, 6, d), 0.0, 0.5),
        'rwkv_w_rkv': nrm((N_RWKV, 3, d, d), d ** -0.5),
        'rwkv_w0': uni((N_RWKV, N_DIR, d), -6.0, -1.0),
        'rwkv_w1': nrm((N_RWKV, N_DIR, d, R_DECAY), d ** -0.5),
        'rwkv_w2': nrm((N_RWKV, N_DIR, R_DECAY, d), 0.1 * R_DECAY ** -0.5),
        'rwkv_a0': nrm((N_RWKV, N_DIR, d), 0.1),
        'rwkv_a1': nrm((N_RWKV, N_DIR, d, R_AAA), d ** -0.5),
        'rwkv_a2': nrm((N_RWKV, N_DIR, R_AAA, d), R_AAA ** -0.5),
        'rwkv_g1': nrm((N_RWKV, d, R_GATE), d ** -0.5),
        'rwkv_g2': nrm((N_RWKV, R_GATE, d), R_GATE ** -0.5),
        'rwkv_k_k': 0.85 + nrm((N_RWKV, d), 0.05),
        'rwkv_k_a': 1.0 + nrm((N_RWKV, d), 0.05),
        'rwkv_r_k': nrm((N_RWKV, N_HEADS, HEAD_DIM), 0.1),
        'rwkv_ln_w': 1.0 + nrm((N_RWKV, d), 0.05),
        'rwkv_ln_b': nrm((N_RWKV, d), 0.01),
        'rwkv_w_o': nrm((N_RWKV, d, d), d ** -0.5),
        'ffn_w_in': nrm((DEPTH, d, 2 * D_FF), d ** -0.5),
        'ffn_conv_w': nrm((DEPTH, CONV_WIDTH, 2 * D_FF), CONV_WIDTH ** -0.5),
        'ffn_conv_b': nrm((DEPTH, 2 * D_FF), 0.01),
        'ffn_w_out': nrm((DEPTH, D_FF, d), D_FF ** -0.5),
    }

def reference(x, norm_mix_g, norm_ffn_g, norm_final_g, fnet_w_o, fnet_b_o, rwkv_mu, rwkv_w_rkv,
              rwkv_w0, rwkv_w1, rwkv_w2, rwkv_a0, rwkv_a1, rwkv_a2, rwkv_g1, rwkv_g2, rwkv_k_k,
              rwkv_k_a, rwkv_r_k, rwkv_ln_w, rwkv_ln_b, rwkv_w_o, ffn_w_in, ffn_conv_w, ffn_conv_b,
              ffn_w_out):
    h = x
    for i in range(DEPTH):
        hn = rms_norm(h, norm_mix_g[i])
        j = i // N_MIXERS
        if i % N_MIXERS == 0:
            h = h + fourier_mixer(hn, fnet_w_o[j], fnet_b_o[j])
        else:
            h = h + rwkv7_mixer(hn, rwkv_mu[j], rwkv_w_rkv[j], rwkv_w0[j], rwkv_w1[j], rwkv_w2[j],
                                rwkv_a0[j], rwkv_a1[j], rwkv_a2[j], rwkv_g1[j], rwkv_g2[j],
                                rwkv_k_k[j], rwkv_k_a[j], rwkv_r_k[j], rwkv_ln_w[j], rwkv_ln_b[j],
                                rwkv_w_o[j])
        h = h + conv_ffn(rms_norm(h, norm_ffn_g[i]), ffn_w_in[i], ffn_conv_w[i], ffn_conv_b[i],
                         ffn_w_out[i])
    return rms_norm(h, norm_final_g)


_drawn_inputs = setup_inputs


def setup_inputs(seed=0):
    import zlib

    import numpy as np

    out = dict(_drawn_inputs(seed))
    spreads = {}
    factors = {'fnet_b_o': 4.031,
     'rwkv_w1': 8.0,
     'rwkv_w2': 8.0,
     'rwkv_a0': 3.952,
     'rwkv_ln_w': 2.882,
     'rwkv_ln_b': 21.933,
     'ffn_conv_b': 5.827}
    for name, (base, spread) in spreads.items():
        noise = np.random.default_rng([zlib.crc32(name.encode()), seed]).standard_normal(out[name].shape)
        drawn = base * np.exp(spread * noise) if base else spread * noise
        out[name] = jnp.asarray(drawn.astype(out[name].dtype))
    for name, factor in factors.items():
        out[name] = (out[name] * factor).astype(out[name].dtype)
    return out
```

```python
from contextlib import ExitStack

import numpy as np

import concourse.bass as bass
from concourse import mybir

F32 = mybir.dt.float32
F32R = mybir.dt.float32r
ALU = mybir.AluOpType
ACT = mybir.ActivationFunctionType
AX = mybir.AxisListType

P = 128
D = 1024
S = 1024
KT = D // P
HALF = 512
GROUPS = 4
GD = D // GROUPS
GT = GD // P
FOLD = S // 2
DFF = 2816
FT = DFF // P
PAIRS = FT // 2
HD = 64
HEADS = D // HD
NZ = 2
CH = 64
NCH = S // CH
RANK = 64
RG = 160
RMS_EPS = 1e-6
GN_EPS = 64e-5
L2_EPS = 1e-12
DECAY_SCALE = float(np.exp(-0.5))


class Buffers:

    def __init__(self, nc, phase, sems):
        self.nc, self.phase, self.used = nc, phase, []
        self.stack = ExitStack()

    def __enter__(self):
        return self

    def __exit__(self, *a):
        if self.used and a[0] is None:
            with self.nc.Block() as block:
                @block.gpsimd
                def _(pool):
                    for sem in self.used:
                        pool.sem_clear(sem)
        self.stack.close()

    def sb(self, name, shape, dt=F32):
        return self.stack.enter_context(self.nc.sbuf_tensor(f"{self.phase}_{name}", shape, dt))

    def ps(self, name, shape, dt=F32):
        return self.stack.enter_context(self.nc.psum_tensor(f"{self.phase}_{name}", shape, dt))

    def sem(self, name):
        self.used.append(self.stack.enter_context(self.nc.semaphore(f"{self.phase}_{name}")))
        return self.used[-1]


def after(eng, sem, count):
    if not (isinstance(count, int) and count <= 0):
        eng.wait_ge(sem, count)


def f32(ap):
    return ap.bitcast(F32)


def three_passes(pe, out, whi, wlo, xhi, xlo, first, last):
    pe.matmul(out, whi, xhi, start=first, stop=False)
    pe.matmul(out, whi, xlo, start=False, stop=False)
    return pe.matmul(out, wlo, xhi, start=False, stop=last)


def fnet_tokens(nc, sems, io, eo_hi, eo_lo, a_hi, a_lo, b_hi, b_lo):
    NC_ = FOLD + 2
    with Buffers(nc, "ft", sems) as b:
        NS = FOLD // P
        x = b.sb("x", [P, D])
        xr = b.sb("xr", [P, D])
        sq = b_hi[:, 0:2, :].rearrange("p a b -> p (a b)")
        t = b.sb("t", [P, 2, D])
        x512 = b.sb("x512", [1, D])
        x512hi = b.sb("x512hi", [1, D], F32R)
        x512lo = b.sb("x512lo", [1, D], F32R)
        stat = b.sb("stat", [P, 4 * (2 * NS + 1)])
        eps = b.sb("eps", [P, 1])
        gain = b.sb("gain", [P, KT])
        tab = b.sb("tab", [P, NS, NC_])
        cs, sn = tab[:, :, :], tab[:, :, 0:FOLD]
        alt = b.sb("alt", [1, NC_])
        cs_hi = b.sb("cs_hi", [P, NS, NC_], F32R)
        cs_lo = b.sb("cs_lo", [P, NS, NC_], F32R)
        sn_hi = b.sb("sn_hi", [P, NS, FOLD], F32R)
        sn_lo = b.sb("sn_lo", [P, NS, FOLD], F32R)
        altr = b.sb("altr", [1, NC_], F32R)
        e_hi, o_hi = eo_hi[:, 0:NS, :], eo_hi[:, NS:2 * NS, :]
        e_lo, o_lo = eo_lo[:, 0:NS, :], eo_lo[:, NS:2 * NS, :]
        pa = b.ps("pa", [P, 2, 2, HALF])
        pb = b.ps("pb", [P, 2, HALF])
        s_x = b.sem("s_x")
        s_tab = [b.sem(f"s_tab{i}") for i in range(2)]
        s_c = b.sem("s_c")
        s_m = b.sem("s_m")
        s_sq = b.sem("s_sq")
        s_mean = b.sem("s_mean")
        s_std = b.sem("s_std")
        s_rstd = b.sem("s_rstd")
        s_xr = b.sem("s_xr")
        s_fold = b.sem("s_fold")
        s_hi = b.sem("s_hi")
        s_lo = b.sem("s_lo")
        s_chi = b.sem("s_chi")
        s_clo = b.sem("s_clo")
        s_mm = b.sem("s_mm")
        s_ehi = b.sem("s_ehi")
        s_elo = b.sem("s_elo")

        def st(kind, j):
            return stat[:, kind * (2 * NS + 1) + j:kind * (2 * NS + 1) + j + 1]

        with nc.Block() as block:

            @block.sync
            def _(sp):
                sp.dma_start(gain[:, :], io["fnet_gain"]).then_inc(s_c, 16)
                sp.dma_start(x512[:, :], io["x_tok"][FOLD:FOLD + 1, :]).then_inc(s_c, 16)
                sp.dma_start(alt[:, :], io["alt"]).then_inc(s_c, 16)
                sp.dma_start(cs, io["cos_tok"].rearrange("(k p) n -> p k n", p=P)).then_inc(s_tab[0], 16)
                for k in range(NS):
                    after(sp, s_fold, 2 * k)
                    sp.dma_start(x[:, :], io["x_tok"][k * P:(k + 1) * P, :]).then_inc(s_x, 16)
                    sp.dma_start(xr[:, :], io["x_mirror"][k * P:(k + 1) * P, :]).then_inc(s_x, 16)
                    if k == 0:
                        sp.wait_ge(s_clo, 1)
                        sp.dma_start(sn, io["sin_tok"].rearrange("(k p) n -> p k n", p=P)).then_inc(s_tab[1], 16)

            @block.gpsimd
            def _(pool):
                pool.memset(eps[:, :], RMS_EPS).then_inc(s_m, 1)
                pool.memset(stat[:, :], 0.0).then_inc(s_m, 1)
                pool.wait_ge(s_chi, 1)
                pool.tensor_tensor(cs_lo[:, :, :], cs, f32(cs_hi[:, :, :]), ALU.subtract).then_inc(s_clo, 1)
                pool.wait_ge(s_chi, 2)
                pool.tensor_tensor(sn_lo[:, :, :], sn, f32(sn_hi[:, :, :]), ALU.subtract).then_inc(s_clo, 1)

            @block.scalar
            def _(act):
                act.wait_ge(s_c, 48)
                act.wait_ge(s_m, 2)
                act.wait_ge(s_tab[0], 16)
                act.copy(cs_hi[:, :, :], cs).then_inc(s_chi, 1)
                act.activation(sq[0:1, :], x512[:, :], ACT.Square, accum_out=stat[0:1, 8:9]).then_inc(s_sq, 1)
                n = 1
                for k in range(NS):
                    act.wait_ge(s_x, 32 * (k + 1))
                    for o, src in ((0, x), (1, xr)):
                        act.wait_ge(s_sq, n)
                        j = 2 * k + o
                        act.activation(sq[:, :], src[:, :], ACT.Square, accum_out=st(0, j)).then_inc(s_sq, 1)
                        n += 1
                    if k == 0:
                        act.wait_ge(s_sq, 3)
                        act.activation(stat[0:1, 17:18], stat[0:1, 8:9], ACT.Sqrt, scale=1.0 / D,
                                       bias=eps[0:1, :]).then_inc(s_std, 1)
                    act.wait_ge(s_sq, n)
                    act.activation(stat[:, 9 + 2 * k:11 + 2 * k], stat[:, 2 * k:2 * k + 2], ACT.Sqrt, scale=1.0 / D,
                                   bias=eps[:, :]).then_inc(s_std, 1)
                    act.wait_ge(s_rstd, k + 2)
                    act.activation(xr[:, :], xr[:, :], ACT.Copy,
                                   scale=st(2, 2 * k + 1)).then_inc(s_xr, 1)
                    act.wait_ge(s_fold, 2 * k + 1)
                    act.copy(e_hi[:, k, :], t[:, 0, :]).then_inc(s_hi, 1)
                    act.wait_ge(s_fold, 2 * k + 2)
                    act.copy(o_hi[:, k, :], t[:, 1, :]).then_inc(s_hi, 1)
                act.wait_ge(s_tab[1], 16)
                act.copy(sn_hi[:, :, :], sn).then_inc(s_chi, 1)
                act.copy(altr[:, :], alt[:, :]).then_inc(s_chi, 1)
                act.wait_ge(s_fold, 2 * NS + 1)
                act.copy(x512hi[:, :], x512[:, :]).then_inc(s_hi, 1)
                for k in range(KT):
                    act.wait_ge(s_mm, k + 1)
                    q = k % 2
                    for hf, lo, w in ((0, 0, 256), (1, 256, 258)):
                        act.activation(a_hi[:, k, lo:lo + w], pa[:, q, hf, 0:w], ACT.Copy,
                                       scale=gain[:, k:k + 1]).then_inc(s_ehi, 1)
                    act.activation(b_hi[:, k, :], pb[:, q, :], ACT.Copy, scale=gain[:, k:k + 1]).then_inc(s_ehi, 1)

            @block.vector
            def _(dve):
                dve.wait_ge(s_std, 1)
                dve.reciprocal(stat[0:1, 26:27], stat[0:1, 17:18]).then_inc(s_rstd, 1)
                for k in range(NS):
                    dve.wait_ge(s_std, k + 2)
                    dve.reciprocal(stat[:, 18 + 2 * k:20 + 2 * k], stat[:, 9 + 2 * k:11 + 2 * k]).then_inc(s_rstd, 1)
                    dve.wait_ge(s_rstd, k + 2)
                    dve.wait_ge(s_xr, k + 1)
                    if k:
                        dve.wait_ge(s_lo, 2 * k)
                    dve.scalar_tensor_tensor(t[:, 0, :], x[:, :], st(2, 2 * k), xr[:, :], ALU.mult,
                                             ALU.add).then_inc(s_fold, 1)
                    dve.scalar_tensor_tensor(t[:, 1, :], x[:, :], st(2, 2 * k), xr[:, :], ALU.mult,
                                             ALU.subtract).then_inc(s_fold, 1)
                    dve.wait_ge(s_hi, 2 * k + 1)
                    dve.wait_ge(s_fold, 2 * k + 2)
                    dve.tensor_tensor(e_lo[:, k, :], t[:, 0, :], f32(e_hi[:, k, :]), ALU.subtract).then_inc(s_lo, 1)
                    dve.wait_ge(s_hi, 2 * k + 2)
                    dve.tensor_tensor(o_lo[:, k, :], t[:, 1, :], f32(o_hi[:, k, :]), ALU.subtract).then_inc(s_lo, 1)
                dve.tensor_scalar(x512[:, :], x512[:, :], stat[0:1, 26:27], None, ALU.mult).then_inc(s_fold, 1)
                dve.wait_ge(s_hi, 2 * NS + 1)
                dve.wait_ge(s_fold, 2 * NS + 1)
                dve.tensor_tensor(x512lo[:, :], x512[:, :], f32(x512hi[:, :]), ALU.subtract).then_inc(s_lo, 1)
                n = 0
                for k in range(KT):
                    q = k % 2
                    for hf, lo, w in ((0, 0, 256), (1, 256, 258)):
                        n += 1
                        dve.wait_ge(s_ehi, n)
                        dve.scalar_tensor_tensor(a_lo[:, k, lo:lo + w], pa[:, q, hf, 0:w], gain[:, k:k + 1],
                                                 f32(a_hi[:, k, lo:lo + w]), ALU.mult, ALU.subtract).then_inc(s_elo, 1)
                    n += 1
                    dve.wait_ge(s_ehi, n)
                    dve.scalar_tensor_tensor(b_lo[:, k, :], pb[:, q, :], gain[:, k:k + 1], f32(b_hi[:, k, :]),
                                             ALU.mult, ALU.subtract).then_inc(s_elo, 1)

            @block.tensor
            def _(pe):
                pe.wait_ge(s_clo, 2)
                pe.wait_ge(s_chi, 3)
                pe.wait_ge(s_lo, 2 * NS + 1)
                for k in range(KT):
                    q = k % 2
                    f = slice(k * P, (k + 1) * P)
                    if k >= 2:
                        pe.wait_ge(s_elo, 3 * (k - 1))
                    for hf, lo, w in ((0, 0, 256), (1, 256, 258)):
                        for j in range(NS):
                            three_passes(pe, pa[:, q, hf, 0:w], e_hi[:, j, f], e_lo[:, j, f],
                                         cs_hi[:, j, lo:lo + w], cs_lo[:, j, lo:lo + w], j == 0, False)
                        pe.matmul(pa[:, q, hf, 0:w], x512hi[:, f], altr[:, lo:lo + w], start=False, stop=False)
                        pe.matmul(pa[:, q, hf, 0:w], x512lo[:, f], altr[:, lo:lo + w], start=False, stop=True)
                    for j in range(NS):
                        mm = three_passes(pe, pb[:, q, :], o_hi[:, j, f], o_lo[:, j, f], sn_hi[:, j, :],
                                          sn_lo[:, j, :], j == 0, j == NS - 1)
                    mm.then_inc(s_mm, 1)


def fnet_features(nc, sems, io, a_hi, a_lo, b_hi, b_lo, y_hi, y_lo):
    with Buffers(nc, "ff", sems) as b:
        cg = b.sb("cg", [P, 2, GT, GD])
        cg_hi = b.sb("cg_hi", [P, 2, GT, GD], F32R)
        cg_lo = b.sb("cg_lo", [P, 2, GT, GD], F32R)
        q_sb = b.sb("q_sb", [P, 2, HALF])
        y = b.sb("y", [P, 2, S])
        pp = b.ps("pp", [P, 2, 2, HALF])
        pq = b.ps("pq", [P, 2, HALF])
        s_c = b.sem("s_c")
        s_chi = b.sem("s_chi")
        s_clo = b.sem("s_clo")
        s_mm = b.sem("s_mm")
        s_q = b.sem("s_q")
        s_y = b.sem("s_y")
        s_yhi = b.sem("s_yhi")
        s_ylo = b.sem("s_ylo")
        with nc.Block() as block:

            @block.sync
            def _(sp):
                sp.dma_start(cg[:, 0, :, :], io["cos_grp"].rearrange("(k p) n -> p k n", p=P)).then_inc(s_c, 16)
                sp.dma_start(cg[:, 1, :, :], io["sin_grp"].rearrange("(k p) n -> p k n", p=P)).then_inc(s_c, 16)

            @block.scalar
            def _(act):
                act.wait_ge(s_c, 32)
                act.copy(cg_hi[:, :, :, :], cg[:, :, :, :]).then_inc(s_chi, 1)
                for n in range(KT):
                    q = n % 2
                    act.wait_ge(s_mm, n + 1)
                    if n >= 2:
                        act.wait_ge(s_y, 5 * (n - 1))
                    act.copy(q_sb[:, q, :], pq[:, q, :]).then_inc(s_q, 1)
                    act.wait_ge(s_y, 5 * (n + 1))
                    act.copy(y_hi[:, n, :], y[:, q, :]).then_inc(s_yhi, 1)

            @block.gpsimd
            def _(pool):
                for n in range(KT):
                    pool.wait_ge(s_yhi, n + 1)
                    pool.tensor_tensor(y_lo[:, n, :], y[:, n % 2, :], f32(y_hi[:, n, :]), ALU.subtract).then_inc(s_ylo, 1)

            @block.vector
            def _(dve):
                dve.wait_ge(s_chi, 1)
                dve.tensor_tensor(cg_lo[:, :, :, :], cg[:, :, :, :], f32(cg_hi[:, :, :, :]),
                                  ALU.subtract).then_inc(s_clo, 1)
                for n in range(KT):
                    q = n % 2
                    dve.wait_ge(s_q, n + 1)
                    if n >= 2:
                        dve.wait_ge(s_ylo, n - 1)
                    for hf in range(2):
                        o = 256 * hf
                        dve.tensor_tensor(y[:, q, o:o + 256], pp[:, q, hf, 0:256], q_sb[:, q, o:o + 256],
                                          ALU.subtract).then_inc(s_y, 1)
                    dve.tensor_copy(y[:, q, FOLD:FOLD + 1], pp[:, q, 1, 256:257]).then_inc(s_y, 1)
                    dve.tensor_tensor(y[:, q, S - 1:S - 256:-1], pp[:, q, 0, 1:256], q_sb[:, q, 1:256],
                                      ALU.add).then_inc(s_y, 1)
                    dve.tensor_tensor(y[:, q, S - 256:FOLD:-1], pp[:, q, 1, 0:256], q_sb[:, q, 256:512],
                                      ALU.add).then_inc(s_y, 1)

            @block.tensor
            def _(pe):
                pe.wait_ge(s_clo, 1)
                for n in range(KT):
                    q, g, m = n % 2, n // GT, n % GT
                    f = slice(m * P, (m + 1) * P)
                    if n >= 2:
                        pe.wait_ge(s_y, 5 * (n - 1))
                    for hf, lo, w in ((0, 0, 256), (1, 256, 258)):
                        for j in range(GT):
                            k = g * GT + j
                            three_passes(pe, pp[:, q, hf, 0:w], cg_hi[:, 0, j, f], cg_lo[:, 0, j, f],
                                         a_hi[:, k, lo:lo + w], a_lo[:, k, lo:lo + w], j == 0, j == GT - 1)
                    for j in range(GT):
                        k = g * GT + j
                        mm = three_passes(pe, pq[:, q, :], cg_hi[:, 1, j, f], cg_lo[:, 1, j, f], b_hi[:, k, :],
                                          b_lo[:, k, :], j == 0, j == GT - 1)
                    mm.then_inc(s_mm, 1)


def project(nc, sems, name, weight, x_hi, x_lo, h=None, residual=None, bias=None, store=None):
    w_view = weight.rearrange("(k p) n -> p k n", p=P)
    with Buffers(nc, name, sems) as b:
        w = b.sb("w", [P, 2, KT, P])
        w_hi = [b.sb(f"w_hi{i}", [P, KT, P], F32R) for i in range(2)]
        w_lo = [b.sb(f"w_lo{i}", [P, KT, P], F32R) for i in range(2)]
        res = b.sb("res", [P, 2, S])
        out = b.sb("out", [P, 2, S])
        bias_sb = b.sb("bias", [P, KT])
        ps = b.ps("ps", [P, 2, 2, HALF])
        s_bias = b.sem("s_bias")
        s_w = [b.sem(f"s_w{i}") for i in range(2)]
        s_res = [b.sem(f"s_res{i}") for i in range(2)]
        s_hi = b.sem("s_hi")
        s_lo = b.sem("s_lo")
        s_mm = b.sem("s_mm")
        s_out = b.sem("s_out")
        s_st = [b.sem(f"s_st{i}") for i in range(2)]
        s_credit = b.sem("s_credit")
        with nc.Block() as block:

            @block.sync
            def _(sp):
                def load(t, u):
                    sp.dma_start(w[:, u, :, :], w_view[:, :, bass.ds(t * P, P)]).then_inc(s_w[u], 16)
                    if residual is not None:
                        sp.dma_start(res[:, u, :], residual[bass.ds(t * P, P), :]).then_inc(s_res[u], 16)

                def put(t, u):
                    sp.wait_ge(s_out, t + 1)
                    sp.dma_start(store[bass.ds(t * P, P), :], out[:, u, :]).then_inc(s_st[u], 16)

                if bias is not None:
                    sp.dma_start(bias_sb[:, :], bias).then_inc(s_bias, 16)
                for u in range(2):
                    load(u, u)
                with sp.Fori(1, KT // 2) as i:
                    for u in range(2):
                        sp.wait_ge(s_lo, 2 * i + u - 1)
                        if residual is not None:
                            sp.wait_ge(s_out, 2 * i + u - 1)
                        load(2 * i + u, u)
                        if store is not None:
                            put(2 * i + u - 2, u)
                if store is not None:
                    for u in range(2):
                        put(KT - 2 + u, u)
                    for u in range(2):
                        sp.wait_ge(s_st[u], 16 * (KT // 2))

            @block.scalar
            def _(act):
                with act.Fori(0, KT // 2) as i:
                    for u in range(2):
                        act.wait_ge(s_w[u], 16 * i + 16)
                        act.wait_ge(s_credit, 2 * i + u + 1)
                        act.copy(w_hi[u][:, :, :], w[:, u, :, :]).then_inc(s_hi, 1)

            @block.gpsimd
            def _(pool):
                with pool.Fori(0, KT // 2) as i:
                    for u in range(2):
                        pool.wait_ge(s_hi, 2 * i + u + 1)
                        pool.tensor_tensor(w_lo[u][:, :, :], w[:, u, :, :], f32(w_hi[u][:, :, :]),
                                           ALU.subtract).then_inc(s_lo, 1)

            @block.tensor
            def _(pe):
                pe.sem_inc(s_credit, 2)
                def tile(t, u):
                    pe.wait_ge(s_lo, t + 1)
                    for hf in range(2):
                        c = slice(hf * HALF, (hf + 1) * HALF)
                        for k in range(KT):
                            mm = three_passes(pe, ps[:, u, hf, :], w_hi[u][:, k, :], w_lo[u][:, k, :],
                                              x_hi[:, k, c], x_lo[:, k, c], k == 0, k == KT - 1)
                        if hf == 0:
                            mm.then_inc(s_mm, 1)
                    mm.then_inc(s_mm, 1)
                    pe.wait_ge(s_mm, 2 * t + 2)
                    pe.sem_inc(s_credit, 1)

                for u in range(2):
                    tile(u, u)
                with pe.Fori(1, KT // 2) as i:
                    for u in range(2):
                        pe.wait_ge(s_out, 2 * i + u - 1)
                        tile(2 * i + u, u)

            @block.vector
            def _(dve):
                def tile(t, u, landed):
                    dve.wait_ge(s_mm, 2 * t + 2)
                    both = ps[:, u, :, :]
                    if residual is None:
                        dst = out[:, u, :].rearrange("p (a b) -> p a b", a=2)
                        dve.tensor_copy(dst, both).then_inc(s_out, 1)
                        return
                    dve.wait_ge(s_res[u], landed)
                    r = res[:, u, :].rearrange("p (a b) -> p a b", a=2)
                    dst = h[:, bass.ds(t, 1), :].rearrange("p o (a b) -> p (o a) b", a=2)
                    if bias is None:
                        dve.tensor_tensor(dst, both, r, ALU.add).then_inc(s_out, 1)
                    else:
                        dve.scalar_tensor_tensor(dst, both, bias_sb[:, bass.ds(t, 1)], r, ALU.add,
                                                 ALU.add).then_inc(s_out, 1)

                if bias is not None:
                    dve.wait_ge(s_bias, 16)
                for u in range(2):
                    tile(u, u, 16)
                with dve.Fori(1, KT // 2) as i:
                    for u in range(2):
                        if store is not None:
                            dve.wait_ge(s_st[u], 16 * i)
                        tile(2 * i + u, u, 16 * i + 16)


def rms_norm(nc, sems, name, h, gain_dram, n_hi=None, n_lo=None, store=None, save=None):
    with Buffers(nc, name, sems) as b:
        sq = b.sb("sq", [P, 2, S])
        ones = b.sb("ones", [P, P])
        eps = b.sb("eps", [P, 1])
        gain = b.sb("gain", [P, KT])
        std = b.sb("std", [P, S])
        rstd = b.sb("rstd", [P, S])
        y = b.sb("y", [P, 2, S])
        ps = b.ps("ps", [P, 2, HALF])
        s_c = b.sem("s_c")
        s_g = b.sem("s_g")
        s_save = b.sem("s_save")
        s_sq = b.sem("s_sq")
        s_mm = b.sem("s_mm")
        s_std = b.sem("s_std")
        s_rstd = b.sem("s_rstd")
        s_y = b.sem("s_y")
        s_hi = b.sem("s_hi")
        s_lo = b.sem("s_lo")
        s_st = [b.sem(f"s_st{i}") for i in range(2)]
        split = n_hi is not None
        with nc.Block() as block:

            @block.sync
            def _(sp):
                sp.dma_start(gain[:, :], gain_dram).then_inc(s_g, 16)
                if save is not None:
                    sp.dma_start(save.rearrange("(k p) n -> p k n", p=P), h[:, :, :]).then_inc(s_save, 16)
                    sp.wait_ge(s_save, 16)
                if store is not None:
                    for k in range(KT):
                        sp.wait_ge(s_y, k + 1)
                        sp.dma_start(store[k * P:(k + 1) * P, :], y[:, k % 2, :]).then_inc(s_st[k % 2], 16)
                    for u in range(2):
                        sp.wait_ge(s_st[u], 16 * (KT // 2))

            @block.gpsimd
            def _(pool):
                pool.memset(ones[:, :], 1.0).then_inc(s_c, 1)
                pool.memset(eps[:, :], RMS_EPS).then_inc(s_c, 1)
                if split:
                    for k in range(KT):
                        pool.wait_ge(s_hi, k + 1)
                        pool.tensor_tensor(n_lo[:, k, :], y[:, k % 2, :], f32(n_hi[:, k, :]),
                                           ALU.subtract).then_inc(s_lo, 1)

            @block.scalar
            def _(act):
                for k in range(KT):
                    if k >= 2:
                        act.wait_ge(s_mm, k - 1)
                    act.activation(sq[:, k % 2, :], h[:, k, :], ACT.Square).then_inc(s_sq, 1)
                act.wait_ge(s_mm, KT)
                act.wait_ge(s_c, 2)
                act.activation(std[:, :].rearrange("p (a b) -> p a b", a=2), ps[:, :, :], ACT.Sqrt, scale=1.0 / D,
                               bias=eps[:, :]).then_inc(s_std, 1)
                if split:
                    for k in range(KT):
                        act.wait_ge(s_y, k + 1)
                        act.copy(n_hi[:, k, :], y[:, k % 2, :]).then_inc(s_hi, 1)

            @block.tensor
            def _(pe):
                pe.wait_ge(s_c, 1)
                for k in range(KT):
                    pe.wait_ge(s_sq, k + 1)
                    for hf in range(2):
                        mm = pe.matmul(ps[:, hf, :], ones[:, :], sq[:, k % 2, hf * HALF:(hf + 1) * HALF],
                                       start=k == 0, stop=k == KT - 1)
                    mm.then_inc(s_mm, 1)

            @block.vector
            def _(dve):
                dve.wait_ge(s_std, 1)
                dve.reciprocal(rstd[:, :], std[:, :]).then_inc(s_rstd, 1)
                dve.wait_ge(s_rstd, 1)
                dve.wait_ge(s_g, 16)
                for k in range(KT):
                    dst = y[:, k % 2, :]
                    if k >= 2 and split:
                        dve.wait_ge(s_lo, k - 1)
                    if k >= 2 and store is not None:
                        dve.wait_ge(s_st[k % 2], 16 * (k // 2))
                    dve.scalar_tensor_tensor(dst, h[:, k, :], gain[:, k:k + 1], rstd[:, :], ALU.mult,
                                             ALU.mult).then_inc(s_y, 1)


def feed_forward(nc, sems, name, h, n_hi, n_lo, w_in, w_out, conv):
    in_view = w_in.rearrange("(k p) n -> p k n", p=P)
    with Buffers(nc, name, sems) as b:
        w = [b.sb(f"w{i}", [P, KT, P]) for i in range(2)]
        w_hi = [[b.sb(f"w_hi{u}{i}", [P, KT, P], F32R) for i in range(2)] for u in range(2)]
        w_lo = [[b.sb(f"w_lo{u}{i}", [P, KT, P], F32R) for i in range(2)] for u in range(2)]
        wo = b.sb("wo", [P, 2, D])
        wo_hi = [b.sb(f"wo_hi{u}", [P, D], F32R) for u in range(2)]
        wo_lo = [b.sb(f"wo_lo{u}", [P, D], F32R) for u in range(2)]
        c = b.sb("c", [P, 2 * FT, 4])
        t = [[b.sb(f"t{u}{i}", [P, S]) for i in range(2)] for u in range(2)]
        a_hi = [b.sb(f"a_hi{u}", [P, S], F32R) for u in range(2)]
        a_lo = [b.sb(f"a_lo{u}", [P, S], F32R) for u in range(2)]
        up = [b.ps(f"up{i}", [P, 2, HALF]) for i in range(2)]
        dn = [b.ps(f"dn{i}", [P, HALF]) for i in range(4)]
        s_c = b.sem("s_c")
        s_w = [b.sem(f"s_w{i}") for i in range(2)]
        s_wo = b.sem("s_wo")
        s_whi = b.sem("s_whi")
        s_wlo = b.sem("s_wlo")
        s_wohi = b.sem("s_wohi")
        s_wolo = b.sem("s_wolo")
        s_up = b.sem("s_up")
        s_tap = b.sem("s_tap")
        s_conv = b.sem("s_conv")
        s_silu = b.sem("s_silu")
        s_prod = b.sem("s_prod")
        s_ahi = b.sem("s_ahi")
        s_alo = b.sem("s_alo")
        s_dn = b.sem("s_dn")
        s_add = b.sem("s_add")

        with nc.Block() as block:

            @block.sync
            def _(sp):
                def load_up(j):
                    for i in range(2):
                        sp.dma_start(w[i][:, :, :], in_view[:, :, bass.ds(j * P + i * DFF, P)]).then_inc(s_w[i], 16)

                def load_down(i):
                    sp.dma_start(wo[:, :, :], w_out[bass.ds(i * 2 * P, 2 * P), :].rearrange(
                        "(u p) n -> p u n", p=P)).then_inc(s_wo, 16)

                sp.dma_start(c[:, :, :], conv).then_inc(s_c, 16)
                load_up(0)
                load_down(0)
                sp.wait_ge(s_wlo, 2)
                load_up(1)
                with sp.Fori(1, PAIRS) as i:
                    sp.wait_ge(s_wlo, 4 * i)
                    load_up(2 * i)
                    sp.wait_ge(s_wolo, 2 * i)
                    load_down(i)
                    sp.wait_ge(s_wlo, 4 * i + 2)
                    load_up(2 * i + 1)

            @block.scalar
            def _(act):
                def split_up(j, u, fresh):
                    for i in range(2):
                        act.wait_ge(s_w[i], 16 * j + 16)
                        if i == 0 and not fresh:
                            act.wait_ge(s_up, 2 * j - 2)
                        act.copy(w_hi[u][i][:, :, :], w[i][:, :, :]).then_inc(s_whi, 1)

                def taps(j, u, fresh):
                    for i in range(2):
                        act.wait_ge(s_up, 2 * j + i + 1)
                        if i == 0 and not fresh:
                            act.wait_ge(s_alo, j - u)
                        k = j + i * FT
                        act.activation(t[u][i][:, :].rearrange("p (a b) -> p a b", a=2), up[i][:, :, :], ACT.Identity,
                                       bias=c[:, bass.ds(k, 1), 3], scale=c[:, bass.ds(k, 1), 1]).then_inc(s_tap, 1)
                    act.wait_ge(s_conv, 4 * j + 2)
                    act.activation(t[u][0][:, :], t[u][0][:, :], ACT.Silu).then_inc(s_silu, 1)

                def commit(i, fresh):
                    if not fresh:
                        act.wait_ge(s_dn, 16 * i)
                    act.wait_ge(s_prod, 2 * i + 2)
                    for u in range(2):
                        act.copy(a_hi[u][:, :], t[u][1][:, :]).then_inc(s_ahi, 1)
                    act.wait_ge(s_wo, 16 * i + 16)
                    for u in range(2):
                        act.copy(wo_hi[u][:, :], wo[:, u, :]).then_inc(s_wohi, 1)

                act.wait_ge(s_c, 16)
                split_up(0, 0, True)
                split_up(1, 1, True)
                taps(0, 0, True)
                split_up(2, 0, False)
                taps(1, 1, True)
                commit(0, True)
                with act.Fori(1, PAIRS - 1) as i:
                    split_up(2 * i + 1, 1, False)
                    taps(2 * i, 0, False)
                    split_up(2 * i + 2, 0, False)
                    taps(2 * i + 1, 1, False)
                    commit(i, False)
                split_up(FT - 1, 1, False)
                taps(FT - 2, 0, False)
                taps(FT - 1, 1, False)
                commit(PAIRS - 1, False)

            @block.gpsimd
            def _(pool):
                def split_up(j, u, fresh):
                    for i in range(2):
                        pool.wait_ge(s_whi, 2 * j + i + 1)
                        pool.tensor_tensor(w_lo[u][i][:, :, :], w[i][:, :, :], f32(w_hi[u][i][:, :, :]),
                                           ALU.subtract).then_inc(s_wlo, 1)

                def commit(i):
                    for u in range(2):
                        pool.wait_ge(s_ahi, 2 * i + u + 1)
                        pool.tensor_tensor(a_lo[u][:, :], t[u][1][:, :], f32(a_hi[u][:, :]),
                                           ALU.subtract).then_inc(s_alo, 1)
                    for u in range(2):
                        pool.wait_ge(s_wohi, 2 * i + u + 1)
                        pool.tensor_tensor(wo_lo[u][:, :], wo[:, u, :], f32(wo_hi[u][:, :]),
                                           ALU.subtract).then_inc(s_wolo, 1)

                split_up(0, 0, True)
                with pool.Fori(0, PAIRS - 1) as i:
                    split_up(2 * i + 1, 1, True)
                    split_up(2 * i + 2, 0, True)
                    commit(i)
                split_up(FT - 1, 1, True)
                commit(PAIRS - 1)

            @block.tensor
            def _(pe):
                def up_product(j, u, fresh):
                    for i in range(2):
                        pe.wait_ge(s_wlo, 2 * j + i + 1)
                        if not fresh:
                            pe.wait_ge(s_conv, 4 * j - 2 + 2 * i)
                        for hf in range(2):
                            cc = slice(hf * HALF, (hf + 1) * HALF)
                            for k in range(KT):
                                mm = three_passes(pe, up[i][:, hf, :], w_hi[u][i][:, k, :], w_lo[u][i][:, k, :],
                                                  n_hi[:, k, cc], n_lo[:, k, cc], k == 0, k == KT - 1)
                        mm.then_inc(s_up, 1)

                def down_product(i, part, fresh):
                    if part == 0:
                        pe.wait_ge(s_alo, 2 * i + 2)
                        pe.wait_ge(s_wolo, 2 * i + 2)
                    for g in range(8 * part, 8 * part + 8):
                        n, hf = g // 2, g % 2
                        cc = slice(hf * HALF, (hf + 1) * HALF)
                        if not (fresh and g < 4):
                            pe.wait_ge(s_add, 16 * i + g - 3)
                        for u in range(2):
                            mm = three_passes(pe, dn[g % 4][:, :], wo_hi[u][:, n * P:(n + 1) * P],
                                              wo_lo[u][:, n * P:(n + 1) * P], a_hi[u][:, cc], a_lo[u][:, cc],
                                              u == 0, u == 1)
                        mm.then_inc(s_dn, 1)

                up_product(0, 0, True)
                up_product(1, 1, False)
                up_product(2, 0, False)
                down_product(0, 0, True)
                up_product(3, 1, False)
                down_product(0, 1, True)
                with pe.Fori(2, PAIRS) as i:
                    up_product(2 * i, 0, False)
                    down_product(i - 1, 0, False)
                    up_product(2 * i + 1, 1, False)
                    down_product(i - 1, 1, False)
                down_product(PAIRS - 1, 0, False)
                down_product(PAIRS - 1, 1, False)

            @block.vector
            def _(dve):
                def convolve(j, u):
                    for i in range(2):
                        k = j + i * FT
                        flat = up[i][:, :, :].rearrange("p a b -> p (a b)")
                        dve.wait_ge(s_tap, 2 * j + i + 1)
                        dve.scalar_tensor_tensor(t[u][i][:, 1:S], flat[:, 0:S - 1], c[:, bass.ds(k, 1), 0],
                                                 t[u][i][:, 1:S], ALU.mult, ALU.add).then_inc(s_conv, 1)
                        dve.wait_ge(s_conv, 4 * j + 2 * i + 1)
                        dve.scalar_tensor_tensor(t[u][i][:, 0:S - 1], flat[:, 1:S], c[:, bass.ds(k, 1), 2],
                                                 t[u][i][:, 0:S - 1], ALU.mult, ALU.add).then_inc(s_conv, 1)

                def gate(j, u):
                    dve.wait_ge(s_silu, j + 1)
                    dve.wait_ge(s_conv, 4 * j + 4)
                    dve.tensor_tensor(t[u][1][:, :], t[u][0][:, :], t[u][1][:, :], ALU.mult).then_inc(s_prod, 1)

                def add(i, part, fresh=False):
                    for g in range(8 * part, 8 * part + 8):
                        n, hf = g // 2, g % 2
                        cc = slice(hf * HALF, (hf + 1) * HALF)
                        dve.wait_ge(s_dn, 16 * i + g + 1)
                        if not fresh:
                            dve.wait_ge(s_add, 16 * i + g - 15)
                        dve.tensor_tensor(h[:, n, cc], dn[g % 4][:, :], h[:, n, cc], ALU.add).then_inc(s_add, 1)

                dve.wait_ge(s_c, 16)
                for u in range(2):
                    convolve(u, u)
                    gate(u, u)
                for u in range(2):
                    convolve(2 + u, u)
                    gate(2 + u, u)
                    add(0, u, True)
                with dve.Fori(2, PAIRS) as i:
                    for u in range(2):
                        convolve(2 * i + u, u)
                        gate(2 * i + u, u)
                        add(i - 1, u)
                for u in range(2):
                    add(PAIRS - 1, u)


def token_mix(nc, sems, name, hn, mu, x_hi, x_lo):
    with Buffers(nc, name, sems) as b:
        m = b.sb("m", [P, KT, 2])
        own = b.sb("own", [P, KT])
        y = b.sb("y", [P, 3, S])
        s_c = b.sem("s_c")
        s_own = b.sem("s_own")
        s_sc = b.sem("s_sc")
        s_y = b.sem("s_y")
        s_hi = b.sem("s_hi")
        s_lo = b.sem("s_lo")
        with nc.Block() as block:

            @block.sync
            def _(sp):
                sp.dma_start(m[:, :, :], mu).then_inc(s_c, 16)

            @block.scalar
            def _(act):
                act.wait_ge(s_own, 2)
                for k in range(KT):
                    after(act, s_lo, k - 2)
                    act.activation(y[:, k % 3, :], hn[:, k, :], ACT.Copy, scale=own[:, k:k + 1]).then_inc(s_sc, 1)
                    if k:
                        act.wait_ge(s_y, 2 * k)
                        act.copy(x_hi[:, k - 1, :], y[:, (k - 1) % 3, :]).then_inc(s_hi, 1)
                act.wait_ge(s_y, 2 * KT)
                act.copy(x_hi[:, KT - 1, :], y[:, (KT - 1) % 3, :]).then_inc(s_hi, 1)

            @block.gpsimd
            def _(pool):
                for k in range(KT):
                    pool.wait_ge(s_hi, k + 1)
                    pool.tensor_tensor(x_lo[:, k, :], y[:, k % 3, :], f32(x_hi[:, k, :]), ALU.subtract).then_inc(s_lo, 1)

            @block.vector
            def _(dve):
                dve.wait_ge(s_c, 16)
                dve.tensor_tensor(own[:, :], m[:, :, 0], m[:, :, 1], ALU.add).then_inc(s_own, 1)
                dve.wait_ge(s_own, 1)
                dve.tensor_scalar(own[:, :], own[:, :], -1.0, 1.0, ALU.mult, ALU.add).then_inc(s_own, 1)
                for k in range(KT):
                    yk = y[:, k % 3, :]
                    dve.wait_ge(s_sc, k + 1)
                    dve.scalar_tensor_tensor(yk[:, 1:S], hn[:, k, 0:S - 1], m[:, k, 0:1], yk[:, 1:S], ALU.mult,
                                             ALU.add).then_inc(s_y, 1)
                    dve.wait_ge(s_y, 2 * k + 1)
                    dve.scalar_tensor_tensor(yk[:, 0:S - 1], hn[:, k, 1:S], m[:, k, 1:2], yk[:, 0:S - 1], ALU.mult,
                                             ALU.add).then_inc(s_y, 1)


def low_rank_down(nc, sems, name, weight, x_hi, x_lo, func, parts):
    n = weight.shape[1]
    with Buffers(nc, name, sems) as b:
        w = b.sb("w", [P, KT, n])
        w_hi = b.sb("w_hi", [P, KT, n], F32R)
        w_lo = b.sb("w_lo", [P, KT, n], F32R)
        y = b.sb("y", [P, 2, S])
        ps = [b.ps(f"ps{i}", [P, 2, HALF]) for i in range(2)]
        s_w = b.sem("s_w")
        s_hi = b.sem("s_hi")
        s_lo = b.sem("s_lo")
        s_mm = b.sem("s_mm")
        s_y = b.sem("s_y")
        s_yhi = b.sem("s_yhi")
        s_ylo = b.sem("s_ylo")
        with nc.Block() as block:

            @block.sync
            def _(sp):
                sp.dma_start(w[:, :, :], weight.rearrange("(k p) n -> p k n", p=P)).then_inc(s_w, 16)

            @block.scalar
            def _(act):
                act.wait_ge(s_w, 16)
                act.copy(w_hi[:, :, :], w[:, :, :]).then_inc(s_hi, 1)
                for i, (lo, m, hi, _lo) in enumerate(parts):
                    act.wait_ge(s_mm, i + 1)
                    act.activation(y[0:m, i, :].rearrange("p (a b) -> p a b", a=2), ps[i][0:m, :, :],
                                   func).then_inc(s_y, 1)
                    act.wait_ge(s_y, i + 1)
                    act.copy(hi, y[0:m, i, :]).then_inc(s_yhi, 1)

            @block.vector
            def _(dve):
                dve.wait_ge(s_hi, 1)
                dve.tensor_tensor(w_lo[:, :, :], w[:, :, :], f32(w_hi[:, :, :]), ALU.subtract).then_inc(s_lo, 1)
                for i, (_first, m, hi, lo) in enumerate(parts):
                    dve.wait_ge(s_yhi, i + 1)
                    dve.tensor_tensor(lo, y[0:m, i, :], f32(hi), ALU.subtract).then_inc(s_ylo, 1)

            @block.tensor
            def _(pe):
                pe.wait_ge(s_lo, 1)
                for i, (first, m, _hi, _lo) in enumerate(parts):
                    for hf in range(2):
                        c = slice(hf * HALF, (hf + 1) * HALF)
                        for k in range(KT):
                            mm = three_passes(pe, ps[i][0:m, hf, :], w_hi[:, k, first:first + m],
                                              w_lo[:, k, first:first + m], x_hi[:, k, c], x_lo[:, k, c], k == 0,
                                              k == KT - 1)
                    mm.then_inc(s_mm, 1)


def prepare(nc, sems, io, scr, hid_w, hid_a, pc):
    (hw_hi, hw_lo), (ha_hi, ha_lo) = hid_w, hid_a
    with Buffers(nc, "prep", sems) as b:
        r_ = [b.sb(f"r{i}", [P, S]) for i in range(2)]
        k_ = [b.sb(f"k{i}", [P, S]) for i in range(2)]
        v_ = [b.sb(f"v{i}", [P, S]) for i in range(2)]
        vf = b.sb("vf", [P, S])
        w2 = b.sb("w2", [P, D])
        a2 = b.sb("a2", [P, D])
        w2_hi = b.sb("w2_hi", [P, D], F32R)
        w2_lo = b.sb("w2_lo", [P, D], F32R)
        a2_hi = b.sb("a2_hi", [P, D], F32R)
        a2_lo = b.sb("a2_lo", [P, D], F32R)
        vec = b.sb("vec", [P, 8, KT])
        blk = b.sb("blk", [P, P])
        idn = b.sb("idn", [P, P])
        reset = b.sb("reset", [P, S])
        sq = b.sb("sq", [P, S])
        inv = b.sb("inv", [P, S])
        kk = b.sb("kk", [P, S])
        sg = b.sb("sg", [P, S])
        ag = b.sb("ag", [P, S])
        lc = b.sb("lc", [P, S])
        ep = b.sb("ep", [P, NCH, CH + 1])
        em = b.sb("em", [P, S])
        kd = b.sb("kd", [P, NZ, S])
        ka = b.sb("ka", [P, S])
        rk = b.sb("rk", [P, S])
        out_ = [b.sb(f"out{i}", [P, NCH, 4, CH]) for i in range(NZ)]
        vt = b.sb("vt", [P, KT, P])
        bon = b.sb("bon", [P, S])
        pw = b.ps("pw", [P, 2, HALF])
        pa = b.ps("pa", [P, 2, HALF])
        pn = b.ps("pn", [P, 2, HALF])
        pv = b.ps("pv", [P, 2, HALF])
        s_in = [b.sem("s_in0"), b.sem("s_in1")]
        s_c = b.sem("s_c")
        s_mem = b.sem("s_mem")
        s_whi = b.sem("s_whi")
        s_wlo = b.sem("s_wlo")
        s_a = b.sem("s_a")
        s_v = b.sem("s_v")
        s_g = b.sem("s_g")
        s_p = b.sem("s_p")
        s_sq = b.sem("s_sq")
        s_o = [b.sem("s_o0"), b.sem("s_o1")]
        s_ov = b.sem("s_ov")
        s_ob = b.sem("s_ob")
        A_SQ, A_NORM, A_SG, A_AG, A_EP, A_EM, A_N = 1, 2, 3, 4, 5, 6, 10
        V_SCAN = (1, 12)
        V_KK, V_KD, V_KT, V_PER = 4, 7, 11, 10
        V_VT, V_RK, V_BON, V_N = (13, 14, 23, 24), 22, 25, 25
        G_VF, G_RT, G_SUM, G_N = 1, 2, 4, 4
        P_W, P_A, P_VT, P_BON, P_N = (1, 5), (2, 6), (3, 4, 7, 8), 9, 9

        def rev(ap, z):
            return ap[:, ::-1] if z else ap

        def chunks(ap):
            return ap.rearrange("p (c t) -> p c t", t=CH)

        with nc.Block() as block:

            @block.sync
            def _(sp):
                sp.dma_start(w2[:, :], io["w2"]).then_inc(s_c, 16)
                sp.dma_start(a2[:, :], io["a2"]).then_inc(s_c, 16)
                sp.dma_start(vec[:, 0:7, :], io["vec"]).then_inc(s_c, 16)

                def load(t):
                    rows = slice(t * P, (t + 1) * P)
                    after(sp, s_v, V_N * (t - 1))
                    after(sp, s_p, P_N * (t - 1))
                    after(sp, s_g, G_N * (t - 1))
                    for dst, src in ((r_, "r"), (k_, "k"), (v_, "v")):
                        sp.dma_start(dst[t % 2][:, :], scr[src][rows, :]).then_inc(s_in[t % 2], 16)

                load(0)
                for t in range(KT):
                    rows = slice(t * P, (t + 1) * P)
                    if t + 1 < KT:
                        load(t + 1)
                    for z in range(NZ):
                        sp.wait_ge(s_v, V_N * t + V_KT + V_PER * z)
                        sp.wait_ge(s_g, G_N * t + G_RT + z)
                        sp.dma_start(scr["abrk"][:, :, z, t, :].rearrange("c p n -> p c n"),
                                     out_[z][:, :, :, :].rearrange("p c f t -> p c (f t)")).then_inc(s_o[z], 16)
                        sp.wait_ge(s_v, V_N * t + V_VT[1 + 2 * z])
                        sp.dma_start(scr["vt"][z, :, rows].rearrange("(a p) n -> p a n", p=P),
                                     vt[:, :, :]).then_inc(s_ov, 16)
                    sp.wait_ge(s_v, V_N * t + V_BON)
                    sp.dma_start(scr["bonus"][rows, :], bon[:, :]).then_inc(s_ob, 16)
                for z in range(NZ):
                    sp.wait_ge(s_o[z], 16 * KT)
                sp.wait_ge(s_ob, 16 * KT)
                sp.wait_ge(s_ov, 16 * NZ * KT)

            @block.gpsimd
            def _(pool):
                pool.memset(blk[:, :], 0.0).then_inc(s_mem, 1)
                pool.memset(idn[:, :], 0.0).then_inc(s_mem, 1)
                pool.memset(reset[:, :], 1.0).then_inc(s_mem, 1)
                pool.memset(ep[:, :, 0:1], 1.0).then_inc(s_mem, 1)
                for hh in range(2):
                    pool.wait_ge(s_mem, 4 + hh)
                    pool.memset(blk[HD * hh:HD * hh + HD, HD * hh:HD * hh + HD], 1.0).then_inc(s_mem, 1)
                pool.wait_ge(s_mem, 6)
                pool.memset(chunks(reset[:, :])[:, :, 0:1], 0.0).then_inc(s_mem, 1)
                pool.affine_select(out=idn[:, :], in_=idn[:, :], compare_op=ALU.not_equal, fill=1.0, base=0,
                                   pattern=[[-1, P]], channel_multiplier=1).then_inc(s_mem, 1)
                pool.wait_ge(s_mem, 8)
                for t in range(KT):
                    r, v = r_[t % 2], v_[t % 2]
                    pool.wait_ge(s_in[t % 2], 48 * (t // 2 + 1))
                    after(pool, s_p, P_N * t)
                    pool.tensor_copy(vf[:, :], v[:, ::-1]).then_inc(s_g, 1)
                    for z in range(NZ):
                        pool.wait_ge(s_a, A_N * t + A_EP + 4 * z)
                        after(pool, s_o[z], 16 * t)
                        pool.tensor_tensor(out_[z][:, :, 1, :], chunks(rev(r[:, :], z)), ep[:, :, 1:CH + 1],
                                           ALU.mult).then_inc(s_g, 1)
                    pool.wait_ge(s_v, V_N * t + V_KD + V_PER)
                    after(pool, s_p, P_N * (t - 1) + P_BON)
                    pool.tensor_tensor(rk[:, :], kd[:, 0, :], kd[:, 1, ::-1], ALU.add).then_inc(s_g, 1)

            @block.scalar
            def _(act):
                act.wait_ge(s_c, 48)
                act.copy(w2_hi[:, :], w2[:, :]).then_inc(s_whi, 1)
                act.copy(a2_hi[:, :], a2[:, :]).then_inc(s_whi, 1)
                for t in range(KT):
                    k = k_[t % 2]
                    act.wait_ge(s_in[t % 2], 48 * (t // 2 + 1))
                    after(act, s_sq, t)
                    act.activation(sq[:, :], k[:, :], ACT.Square, scale=vec[:, 0, t:t + 1]).then_inc(s_a, 1)
                    act.wait_ge(s_sq, t + 1)
                    after(act, s_v, V_N * (t - 1) + V_KK)
                    act.activation(inv[:, :].rearrange("p (a b) -> p a b", a=2), pa[:, :, :], ACT.Sqrt).then_inc(s_a, 1)
                    for z in range(NZ):
                        act.wait_ge(s_p, P_N * t + P_W[z])
                        after(act, s_v, V_N * t + V_SCAN[0] if z else V_N * (t - 1) + V_SCAN[1])
                        for hf in range(2):
                            dst = sg[:, hf * HALF:(hf + 1) * HALF] if z == 0 else sg[:, ::-1][:, hf * HALF:(hf + 1) * HALF]
                            i_ = act.activation(dst, pw[:, hf, :], ACT.Sigmoid, bias=vec[:, 3 + z, t:t + 1])
                        i_.then_inc(s_a, 1)
                        act.wait_ge(s_p, P_N * t + P_A[z])
                        after(act, s_v, V_N * t + V_KD + V_PER * (z - 1) if z else V_N * (t - 1) + V_KD + V_PER)
                        for hf in range(2):
                            dst = ag[:, hf * HALF:(hf + 1) * HALF] if z == 0 else ag[:, ::-1][:, hf * HALF:(hf + 1) * HALF]
                            i_ = act.activation(dst, pa[:, hf, :], ACT.Sigmoid, bias=vec[:, 5 + z, t:t + 1])
                        i_.then_inc(s_a, 1)
                        act.wait_ge(s_v, V_N * t + V_SCAN[z])
                        after(act, s_g, G_N * t + G_RT + z - 1 if z else G_N * (t - 1) + G_RT + 1)
                        act.activation(ep[:, :, 1:CH + 1], chunks(lc[:, :]), ACT.Exp, scale=-DECAY_SCALE).then_inc(s_a, 1)
                        act.activation(em[:, :], lc[:, :], ACT.Exp, scale=DECAY_SCALE).then_inc(s_a, 1)

            @block.vector
            def _(dve):
                dve.wait_ge(s_whi, 2)
                dve.tensor_tensor(w2_lo[:, :], w2[:, :], f32(w2_hi[:, :]), ALU.subtract).then_inc(s_wlo, 1)
                dve.tensor_tensor(a2_lo[:, :], a2[:, :], f32(a2_hi[:, :]), ALU.subtract).then_inc(s_wlo, 1)
                dve.wait_ge(s_c, 48)
                dve.tensor_scalar(vec[:, 7, :], vec[:, 1, :], -1.0, 1.0, ALU.mult, ALU.add).then_inc(s_wlo, 1)
                dve.wait_ge(s_wlo, 3)
                dve.wait_ge(s_mem, 8)
                for t in range(KT):
                    n = [V_N * t]

                    def step(ins, n=n):
                        n[0] += 1
                        ins.then_inc(s_v, 1)
                        dve.wait_ge(s_v, n[0])

                    r, k, v = r_[t % 2], k_[t % 2], v_[t % 2]
                    for z in range(NZ):
                        kz, kkz, out = rev(k[:, :], z), rev(kk[:, :], z), out_[z]

                        def turned(j):
                            dve.wait_ge(s_p, P_N * t + P_VT[j])
                            if j % 2 == 0:
                                after(dve, s_ov, 16 * (2 * t + j // 2))
                            step(dve.tensor_copy(vt[:, 4 * (j % 2):4 * (j % 2) + 4, :],
                                                 pv[:, j % 2, :].rearrange("p (a n) -> p a n", a=4)))

                        dve.wait_ge(s_a, A_N * t + A_SG + 4 * z)
                        after(dve, s_a, A_N * t + A_EM + 4 * (z - 1) if z else A_N * (t - 1) + A_EM + 4)
                        step(dve.tensor_tensor_scan(lc[:, :], reset[:, :], sg[:, :], 0.0, ALU.mult, ALU.add))
                        if z == 0:
                            step(dve.tensor_scalar(inv[:, :], inv[:, :], L2_EPS, None, ALU.max))
                            step(dve.reciprocal(inv[:, :], inv[:, :]))
                            step(dve.scalar_tensor_tensor(kk[:, :], k[:, :], vec[:, 0, t:t + 1], inv[:, :], ALU.mult,
                                                          ALU.mult))
                        else:
                            turned(0)
                            turned(1)
                        dve.wait_ge(s_a, A_N * t + A_AG + 4 * z)
                        step(dve.tensor_tensor(ka[:, :], kkz, ag[:, :], ALU.mult))
                        step(dve.tensor_scalar(ag[:, :], ag[:, :], vec[:, 1, t:t + 1], vec[:, 7, t:t + 1], ALU.mult,
                                               ALU.add))
                        after(dve, s_g, G_N * t)
                        step(dve.tensor_tensor(kd[:, z, :], kz, ag[:, :], ALU.mult))
                        dve.wait_ge(s_a, A_N * t + A_EM + 4 * z)
                        after(dve, s_o[z], 16 * t)
                        step(dve.scalar_tensor_tensor(out[:, :, 0, :], chunks(kkz), -1.0, ep[:, :, 0:CH], ALU.mult,
                                                      ALU.mult))
                        step(dve.tensor_copy(pc[:, :, z * KT + t], ep[:, :, CH]))
                        step(dve.tensor_tensor(out[:, :, 2, :], chunks(ka[:, :]), chunks(em[:, :]), ALU.mult))
                        step(dve.tensor_tensor(out[:, :, 3, :], chunks(kd[:, z, :]), chunks(em[:, :]), ALU.mult))
                    dve.wait_ge(s_g, G_N * t + G_SUM)
                    step(dve.scalar_tensor_tensor(rk[:, :], r[:, :], vec[:, 2, t:t + 1], rk[:, :], ALU.mult, ALU.mult))
                    turned(2)
                    turned(3)
                    dve.wait_ge(s_p, P_N * t + P_BON)
                    after(dve, s_ob, 16 * t)
                    step(dve.tensor_tensor(bon[:, :].rearrange("p (a b) -> p a b", a=2), pn[:, :, :],
                                           v[:, :].rearrange("p (a b) -> p a b", a=2), ALU.mult))

            @block.tensor
            def _(pe):
                pe.wait_ge(s_mem, 8)
                pe.wait_ge(s_wlo, 2)

                def squares(t):
                    pe.wait_ge(s_a, A_N * t + A_SQ)
                    for hf in range(2):
                        mm = pe.matmul(pa[:, hf, :], blk[:, :], sq[:, hf * HALF:(hf + 1) * HALF], start=True, stop=True)
                    mm.then_inc(s_sq, 1)

                def turn(t, j):
                    pe.wait_ge(s_g, G_N * t + G_VF)
                    src = v_[t % 2] if j < 2 else vf
                    after(pe, s_v, V_N * t + V_VT[j - 2] if j >= 2 else V_N * (t - 1) + V_VT[2 + j])
                    for q in range(4):
                        tok = (4 * (j % 2) + q) * P
                        mm = pe.transpose(pv[:, j % 2, q * P:(q + 1) * P], src[:, tok:tok + P], idn[:, :])
                    mm.then_inc(s_p, 1)

                squares(0)
                for t in range(KT):
                    f = slice(t * P, (t + 1) * P)
                    for z in range(NZ):
                        zp = slice(RANK * z, RANK * (z + 1))
                        for ps, hi, lo, hh, hl, used in ((pw, w2_hi, w2_lo, hw_hi, hw_lo, A_SG),
                                                         (pa, a2_hi, a2_lo, ha_hi, ha_lo, A_AG)):
                            if z:
                                pe.wait_ge(s_a, A_N * t + used)
                            elif used == A_AG:
                                pe.wait_ge(s_a, A_N * t + A_NORM)
                            else:
                                after(pe, s_a, A_N * (t - 1) + used + 4)
                            for hf in range(2):
                                c = slice(hf * HALF, (hf + 1) * HALF)
                                mm = three_passes(pe, ps[:, hf, :], hi[zp, f], lo[zp, f], hh[zp, c], hl[zp, c],
                                                  True, True)
                            mm.then_inc(s_p, 1)
                        turn(t, 2 * z)
                        turn(t, 2 * z + 1)
                    if t + 1 < KT:
                        squares(t + 1)
                    pe.wait_ge(s_v, V_N * t + V_RK)
                    for hf in range(2):
                        mm = pe.matmul(pn[:, hf, :], blk[:, :], rk[:, hf * HALF:(hf + 1) * HALF], start=True, stop=True)
                    mm.then_inc(s_p, 1)


def recurrence(nc, sems, scr, pc):
    NP = NZ * KT
    NB = CH // 16
    with Buffers(nc, "wkv", sems) as b:
        G = [b.sb(f"G{i}", [P, NP, 2, 2, CH], F32) for i in range(2)]
        BK = [b.sb(f"BK{i}", [P, NP, 2, CH]) for i in range(2)]
        SV = [b.sb(f"SV{i}", [P, NP, 2, HD]) for i in range(2)]
        UV = [b.sb(f"UV{i}", [P, NP, 2, HD]) for i in range(2)]
        LR = [b.sb(f"LR{i}", [P, NP, 3, CH]) for i in range(2)]
        BT = [b.sb(f"BT{i}", [P, NP, 2, HD]) for i in range(2)]
        TT = [b.sb(f"TT{i}", [P, NP, CH]) for i in range(2)]
        sub = b.sb("sub", [P, 16, 16])
        inv = b.sb("inv", [P, 16, 16])
        invt = b.sb("invt", [P, 16, 16])
        prod = b.sb("prod", [P, 16, 16])
        DI = b.sb("DI", [P, NP, CH])
        DIt = b.sb("DIt", [P, NP, CH])
        F = b.sb("F", [P, NP, CH])
        M = b.sb("M", [P, NP, CH])
        Mt = b.sb("Mt", [P, NP, CH])
        M2 = b.sb("M2", [P, NP, CH])
        Z = b.sb("Z", [P, NP, CH])
        X = b.sb("X", [P, NP, HD])
        Y = b.sb("Y", [P, NP, CH])
        St = b.sb("St", [P, NP, HD])
        sum_ = b.sb("sum", [P, NP, HD])
        idn = b.sb("idn", [P, P])
        mask = b.sb("mask", [P, 2, CH])
        off = b.sb("off", [P, CH])
        pg = b.ps("pg", [P, 2, 4, P])
        pm = b.ps("pm", [P, 2, 8, CH])
        pq = b.ps("pq", [P, 2, 8, CH])
        py = b.ps("py", [P, 2, 8, CH])
        names = ("mem", "ld0", "ld1", "vt0", "vt1", "gram", "tri", "tr", "bt", "wr", "rd", "sub", "inv",
                 "iw", "ir", "f", "pe_m", "mt", "m", "pe_z", "m2", "z", "tt", "pe_m2", "pe_tt", "pe_x", "x", "pe_u", "u",
                 "vc", "go", "pool_go", "pe_s", "sum", "st", "sv", "pe_y", "y", "yst")
        s = {n: b.sem(f"s_{n}") for n in names}

        HL = slice(0, HD)
        HH = slice(HD, P)
        half = (HL, HH)
        other = (HH, HL)

        def steps(eng, body):
            body(0, 0)
            body(1, 1)
            with eng.Fori(1, NCH // 2) as i:
                body(2 * i, 0)
                body(2 * i + 1, 1)

        with nc.Block() as block:

            @block.sync
            def _(sp):
                def load(n, q):
                    after(sp, s["pe_x"], 2 * n - 2)
                    after(sp, s["pe_y"], 2 * n - 2)
                    after(sp, s["pe_s"], 2 * n - 2)
                    after(sp, s["tr"], 4 * n - 4)
                    src = scr["abrk"][bass.ds(n, 1), :, :, :, :].rearrange("c p z t (f x) -> p (c z t) f x", f=4)
                    for hh in range(2):
                        hp = half[hh]
                        sp.dma_start(G[q][hp, :, hh, :, :], src[hp, :, 0:2, :]).then_inc(s[f"ld{q}"], 16)
                        for f in range(2):
                            sp.dma_start(BK[q][hp, :, (f + hh) % 2, :], src[hp, :, 2 + f, :]).then_inc(s[f"ld{q}"], 16)
                        vsrc = scr["vt"][:, bass.ds(n * CH, CH), :].rearrange("z s (t h i) -> s z t h i", t=KT, h=2)
                        for z in range(NZ):
                            sp.dma_start(SV[q][other[hh], z * KT:(z + 1) * KT, hh, :],
                                         vsrc[:, z, :, hh, :]).then_inc(s[f"vt{q}"], 16)

                def exchange(n, q):
                    for hh in range(2):
                        sp.wait_ge(s["tri"], 16 * n + 8 + 8 * hh)
                        for k in range(NB):
                            p0 = HD * hh + 16 * k
                            sp.dma_start(scr["blocks"][hh, k].rearrange("j s t -> s j t"),
                                         LR[q][p0:p0 + 16, :, 0, 16 * k:16 * k + 16]).then_inc(s["wr"], 16)
                    sp.wait_ge(s["wr"], 128 * n + 128)
                    after(sp, s["inv"], n)
                    sp.dma_start(sub[:, :, :].rearrange("p s t -> p (s t)"),
                                 scr["blocks"].rearrange("h k j s t -> (h k j) (s t)")).then_inc(s["rd"], 16)
                    sp.wait_ge(s["inv"], n + 1)
                    sp.dma_start(scr["inverse"].rearrange("h k j s t -> (h k j) (s t)"),
                                 inv[:, :, :].rearrange("p s t -> p (s t)")).then_inc(s["iw"], 16)
                    sp.dma_start(scr["inverse_t"].rearrange("h k j s t -> (h k j) (s t)"),
                                 invt[:, :, :].rearrange("p s t -> p (s t)")).then_inc(s["iw"], 16)
                    sp.wait_ge(s["iw"], 32 * n + 32)
                    after(sp, s["pe_tt"], 2 * n)
                    after(sp, s["z"], 2 * n)
                    for dst, src in ((DI, "inverse"), (DIt, "inverse_t")):
                        for hh in range(2):
                            for k in range(NB):
                                p0 = HD * hh + 16 * k
                                sp.dma_start(dst[p0:p0 + 16, :, 16 * k:16 * k + 16],
                                             scr[src][hh, k].rearrange("j s t -> s j t")).then_inc(s["ir"], 16)

                def store(n):
                    sp.wait_ge(s["y"], 2 * n + 2)
                    sp.dma_start(scr["y"][bass.ds(n, 1), :, :, :].rearrange("c p j t -> (c p) j t"),
                                 Y[:, :, :]).then_inc(s["yst"], 16)

                load(0, 0)
                exchange(0, 0)
                load(1, 1)
                exchange(1, 1)
                store(0)
                with sp.Fori(1, NCH // 2) as i:
                    load(2 * i, 0)
                    exchange(2 * i, 0)
                    store(2 * i - 1)
                    load(2 * i + 1, 1)
                    exchange(2 * i + 1, 1)
                    store(2 * i)
                store(NCH - 1)
                sp.wait_ge(s["yst"], 16 * NCH)

            @block.gpsimd
            def _(pool):
                pool.memset(idn[:, :], 0.0).then_inc(s["mem"], 1)
                pool.memset(mask[:, :, :], 1.0).then_inc(s["mem"], 1)
                pool.memset(off[:, :], 1.0).then_inc(s["mem"], 1)
                pool.memset(inv[:, :, :], 0.0).then_inc(s["mem"], 1)
                pool.memset(DI[:, :, :], 0.0).then_inc(s["mem"], 1)
                pool.memset(DIt[:, :, :], 0.0).then_inc(s["mem"], 1)
                pool.memset(St[:, :, :], 0.0).then_inc(s["mem"], 1)
                done = [7]

                def ordered(make):
                    pool.wait_ge(s["mem"], done[0])
                    make().then_inc(s["mem"], 1)
                    done[0] += 1

                for hh in range(2):
                    ordered(lambda hh=hh: pool.memset(SV[0][half[hh], :, hh, :], 0.0))
                    for q in range(2):
                        ordered(lambda hh=hh, q=q: pool.memset(LR[q][other[hh], :, 1 + hh, :], 0.0))
                ordered(lambda: pool.affine_select(out=idn[:, :], in_=idn[:, :], compare_op=ALU.not_equal, fill=1.0,
                                                   base=0, pattern=[[-1, P]], channel_multiplier=1))
                ordered(lambda: pool.affine_select(out=inv[:, :, :], in_=inv[:, :, :], compare_op=ALU.not_equal,
                                                   fill=1.0, base=0, pattern=[[-1, 16], [1, 16]],
                                                   channel_multiplier=0))
                for hh in range(2):
                    for f in range(2):
                        mk = mask[HD * hh:HD * hh + HD, f, :]
                        ordered(lambda mk=mk, f=f: pool.affine_select(
                            out=mk, in_=mk, compare_op=ALU.is_ge, fill=0.0, base=f - 1, pattern=[[1, CH]],
                            channel_multiplier=-1))
                for hh in range(2):
                    mk = off[HD * hh:HD * hh + HD, :].rearrange("p (a b) -> p a b", b=16)
                    ordered(lambda mk=mk: pool.affine_select(
                        out=mk, in_=mk, compare_op=ALU.is_ge, fill=0.0, base=-1, pattern=[[16, NB], [0, 16]],
                        channel_multiplier=-1))
                pool.wait_ge(s["mem"], 21)

                def body(n, q):
                    after(pool, s["f"], n)
                    pool.wait_ge(s[f"vt{q}"], 64 * (n // 2) + 64 if isinstance(n, int) else 32 * (n - q) + 64)
                    after(pool, s["pe_y"], 2 * n - 2)
                    pool.sem_inc(s["pool_go"], 1)
                    for hh in range(2):
                        if hh:
                            pool.wait_ge(s["vc"], 2 * n + 1)
                            pool.sem_inc(s["pool_go"], 1)
                        pool.tensor_copy(UV[q][other[hh], :, hh, :], SV[q][other[hh], :, hh, :]).then_inc(s["vc"], 1)
                    pool.wait_ge(s["vc"], 2 * n + 2)
                    pool.wait_ge(s["tri"], 16 * n + 16)
                    after(pool, s["pe_m"], 4 * n)
                    pool.tensor_tensor(F[:, :, :], LR[q][:, :, 0, :],
                                       off[:, :].unsqueeze(1).to_broadcast([P, NP, CH]), ALU.mult).then_inc(s["f"], 1)

                steps(pool, body)

            @block.tensor
            def _(pe):
                pe.wait_ge(s["mem"], 21)

                def settle():
                    pe.sem_inc(s["go"], 1)

                def gram(n, q, done):
                    pe.wait_ge(s[f"ld{q}"], done)
                    for g in range(8):
                        hh, j0 = g // 4, 4 * (g % 4)
                        after(pe, s["tri"], 16 * n + 2 * g - 2)
                        for k in range(4):
                            mm = pe.matmul(pg[:, g % 2, k, :], BK[q][half[hh], j0 + k, :, :],
                                           G[q][half[hh], j0 + k, hh, :, :], start=True, stop=True)
                        mm.then_inc(s["gram"], 1)

                def turn(n, q):
                    for g in range(4):
                        hh, j0 = g // 2, 8 * (g % 2)
                        after(pe, s["y"], 2 * n - 1 + g % 2 if g < 2 else 0)
                        after(pe, s["bt"], 4 * n + g - 1)
                        settle()
                        for k in range(8):
                            mm = pe.transpose(py[:, g % 2, k, :],
                                              BK[q][half[hh], j0 + k, :, :].rearrange("p f t -> p (f t)"),
                                              idn[half[hh], half[hh]])
                        mm.then_inc(s["tr"], 1)

                def small(out, lhs, rhs):
                    settle()
                    for hh in range(2):
                        for k in range(8):
                            mm = pe.matmul(out(half[hh], k), lhs(half[hh], k), rhs(half[hh], k), start=True, stop=True)
                    return mm

                def merge(n, q):
                    pe.wait_ge(s["ir"], 256 * n + 256)
                    pe.wait_ge(s["f"], n + 1)
                    for g in range(2):
                        after(pe, s["tt"], 2 * n + g - 1)
                        small(lambda h, k: pm[h, g, k, :], lambda h, k: F[h, 8 * g + k, :],
                              lambda h, k: DI[h, 8 * g + k, :]).then_inc(s["pe_m"], 1)
                    for g in range(2):
                        pe.wait_ge(s["m"], 2 * n + g + 1)
                        small(lambda h, k: pm[h, g, k, :], lambda h, k: DI[h, 8 * g + k, :],
                              lambda h, k: F[h, 8 * g + k, :]).then_inc(s["pe_m"], 1)
                    for g in range(2):
                        pe.wait_ge(s["mt"], 2 * n + g + 1)
                        small(lambda h, k: pm[h, g, k, :], lambda h, k: Mt[h, 8 * g + k, :],
                              lambda h, k: M[h, 8 * g + k, :]).then_inc(s["pe_m2"], 1)
                    for g in range(2):
                        pe.wait_ge(s["m2"], 2 * n + g + 1)
                        small(lambda h, k: pm[h, g, k, :], lambda h, k: M[h, 8 * g + k, :],
                              lambda h, k: DIt[h, 8 * g + k, :]).then_inc(s["pe_z"], 1)
                    for g in range(2):
                        pe.wait_ge(s["z"], 2 * n + g + 1)
                        small(lambda h, k: pm[h, g, k, :], lambda h, k: M2[h, 8 * g + k, :],
                              lambda h, k: Z[h, 8 * g + k, :]).then_inc(s["pe_tt"], 1)

                def advance(n, q, landed):
                    pe.wait_ge(s[f"vt{q}"], landed)
                    after(pe, s["sv"], 4 * n)
                    for g in range(2):
                        after(pe, s["sum"], 2 * n + g - 1)
                        for hh in range(2):
                            for k in range(8):
                                j = 8 * g + k
                                mm = pe.matmul(pq[half[hh], g, k, :], G[q][:, j, hh, 0, :], SV[q][:, j, hh, :],
                                               start=True, stop=True)
                        mm.then_inc(s["pe_x"], 1)
                    for g in range(2):
                        pe.wait_ge(s["x"], 2 * n + g + 1)
                        pe.wait_ge(s["tt"], 2 * n + g + 1)
                        small(lambda h, k: pq[h, g, k, :], lambda h, k: TT[q][h, 8 * g + k, :],
                              lambda h, k: X[h, 8 * g + k, :]).then_inc(s["pe_u"], 1)
                    for g in range(2):
                        pe.wait_ge(s["u"], 4 * n + 2 * g + 2)
                        pe.wait_ge(s["vc"], 2 * n + 2)
                        pe.wait_ge(s["bt"], 4 * n + 4)
                        for hh in range(2):
                            for k in range(8):
                                j = 8 * g + k
                                mm = pe.matmul(pq[half[hh], g, k, :], BT[q][:, j, hh, :], UV[q][:, j, hh, :],
                                               start=True, stop=True)
                        mm.then_inc(s["pe_s"], 1)
                    for g in range(2):
                        after(pe, s["y"], 2 * n + g - 1)
                        pe.wait_ge(s["bt"], 4 * n + 4)
                        for hh in range(2):
                            for k in range(8):
                                j = 8 * g + k
                                pe.matmul(py[half[hh], g, k, :], SV[q][:, j, hh, :], G[q][:, j, hh, 1, :], start=True,
                                          stop=False)
                                mm = pe.matmul(py[half[hh], g, k, :], UV[q][:, j, hh, :], LR[q][:, j, 1 + hh, :],
                                               start=False, stop=True)
                        mm.then_inc(s["pe_y"], 1)

                gram(0, 0, 96)
                turn(0, 0)
                merge(0, 0)

                def body(n, q, landed, v_landed):
                    gram(n + 1, 1 - q, landed)
                    advance(n, q, v_landed)
                    turn(n + 1, 1 - q)
                    merge(n + 1, 1 - q)

                body(0, 0, 96, 64)
                body(1, 1, 192, 64)
                with pe.Fori(1, NCH // 2 - 1) as i:
                    body(2 * i, 0, 96 * i + 96, 64 * i + 64)
                    body(2 * i + 1, 1, 96 * i + 192, 64 * i + 64)
                body(NCH - 2, 0, 96 * (NCH // 2), 64 * (NCH // 2))
                advance(NCH - 1, 1, 64 * (NCH // 2))

            @block.scalar
            def _(act):
                def turned(n, q):
                    for g in range(4):
                        hh, j0 = g // 2, 8 * (g % 2)
                        act.wait_ge(s["tr"], 4 * n + g + 1)
                        after(act, s["pe_s"], 2 * n - 2)
                        act.copy(BT[q][:, j0:j0 + 8, hh, :], py[:, g % 2, :, :]).then_inc(s["bt"], 1)

                def merged(n, q):
                    for g in range(2):
                        gs = slice(8 * g, 8 * g + 8)
                        act.wait_ge(s["pe_m"], 4 * n + g + 1)
                        after(act, s["pe_z"], 2 * n)
                        act.copy(M[:, gs, :], pm[:, g, :, :]).then_inc(s["m"], 1)
                    for g in range(2):
                        gs = slice(8 * g, 8 * g + 8)
                        act.wait_ge(s["pe_m"], 4 * n + g + 3)
                        act.copy(Mt[:, gs, :], pm[:, g, :, :]).then_inc(s["mt"], 1)
                    for g in range(2):
                        gs = slice(8 * g, 8 * g + 8)
                        act.wait_ge(s["pe_m2"], 2 * n + g + 1)
                        after(act, s["pe_tt"], 2 * n)
                        act.copy(M2[:, gs, :], pm[:, g, :, :]).then_inc(s["m2"], 1)

                def advanced(n, q):
                    for g in range(2):
                        gs = slice(8 * g, 8 * g + 8)
                        act.wait_ge(s["pe_x"], 2 * n + g + 1)
                        act.copy(X[:, gs, :], pq[:, g, :, :]).then_inc(s["x"], 1)
                    for g in range(2):
                        gs = slice(8 * g, 8 * g + 8)
                        act.wait_ge(s["pe_u"], 2 * n + g + 1)
                        after(act, s["pe_y"], 2 * n - 2)
                        for hh in range(2):
                            act.copy(UV[q][half[hh], gs, hh, :], pq[half[hh], g, :, :]).then_inc(s["u"], 1)
                    for g in range(2):
                        gs = slice(8 * g, 8 * g + 8)
                        act.wait_ge(s["st"], 2 * n + g + 1)
                        after(act, s["pe_y"], 2 * n)
                        for hh in range(2):
                            act.copy(SV[1 - q][half[hh], gs, hh, :], St[half[hh], gs, :]).then_inc(s["sv"], 1)
                    for g in range(2):
                        gs = slice(8 * g, 8 * g + 8)
                        act.wait_ge(s["pe_y"], 2 * n + g + 1)
                        after(act, s["yst"], 16 * n)
                        act.copy(Y[:, gs, :], py[:, g, :, :]).then_inc(s["y"], 1)

                turned(0, 0)
                merged(0, 0)

                def body(n, q):
                    advanced(n, q)
                    turned(n + 1, 1 - q)
                    merged(n + 1, 1 - q)

                body(0, 0)
                body(1, 1)
                with act.Fori(1, NCH // 2 - 1) as i:
                    body(2 * i, 0)
                    body(2 * i + 1, 1)
                body(NCH - 2, 0)
                advanced(NCH - 1, 1)

            @block.vector
            def _(dve):
                dve.wait_ge(s["mem"], 21)

                def triangles(n, q):
                    after(dve, s["pe_y"], 2 * n - 2)
                    for g in range(8):
                        hh, j0 = g // 4, 4 * (g % 4)
                        dve.wait_ge(s["gram"], 8 * n + g + 1)
                        for part, dst in ((other[hh], G[q][other[hh], j0:j0 + 4, hh, :, :]),
                                          (half[hh], LR[q][half[hh], j0:j0 + 4, 0:2 + hh:1 + hh, :])):
                            mk = mask[part, :, :].unsqueeze(1).to_broadcast([HD, 4, 2, CH])
                            dve.tensor_tensor(dst, pg[part, g % 2, :, :].rearrange("p j (f t) -> p j f t", f=2), mk,
                                              ALU.mult).then_inc(s["tri"], 1)

                def substitute(n, q):
                    dve.wait_ge(s["rd"], 16 * n + 16)
                    after(dve, s["iw"], 32 * n)
                    for t in range(1, 16):
                        after(dve, s["sub"], 30 * n + 2 * (t - 1))
                        dve.tensor_tensor(prod[:, 0:t, 0:t], inv[:, 0:t, 0:t].rearrange("p s j -> p j s"),
                                          sub[:, 0:t, t:t + 1].rearrange("p s o -> p o s").to_broadcast([P, t, t]),
                                          ALU.mult).then_inc(s["sub"], 1)
                        dve.wait_ge(s["sub"], 30 * n + 2 * t - 1)
                        dve.tensor_reduce(inv[:, t, 0:t], prod[:, 0:t, 0:t], AX.X, ALU.add).then_inc(s["sub"], 1)
                    dve.wait_ge(s["sub"], 30 * n + 30)
                    dve.tensor_copy(invt[:, :, :], inv[:, :, :].rearrange("p t j -> p j t")).then_inc(s["inv"], 1)

                def merged(n, q):
                    for g in range(2):
                        gs = slice(8 * g, 8 * g + 8)
                        dve.wait_ge(s["pe_z"], 2 * n + g + 1)
                        dve.tensor_tensor(Z[:, gs, :], pm[:, g, :, :], DIt[:, gs, :], ALU.add).then_inc(s["z"], 1)
                    for g in range(2):
                        gs = slice(8 * g, 8 * g + 8)
                        dve.wait_ge(s["pe_tt"], 2 * n + g + 1)
                        after(dve, s["pe_u"], 2 * n - 2)
                        dve.tensor_tensor(TT[q][:, gs, :], pm[:, g, :, :], Z[:, gs, :], ALU.add).then_inc(s["tt"], 1)

                def advanced(n, q):
                    for g in range(2):
                        gs = slice(8 * g, 8 * g + 8)
                        dve.wait_ge(s["pe_s"], 2 * n + g + 1)
                        after(dve, s["st"], 2 * n + g - 1)
                        dve.tensor_tensor(sum_[:, gs, :], pq[:, g, :, :], St[:, gs, :], ALU.add).then_inc(s["sum"], 1)
                        dve.wait_ge(s["sum"], 2 * n + g + 1)
                        after(dve, s["sv"], 4 * n)
                        decay = pc[:, bass.ds(n, 1), gs].rearrange("p c j -> p (c j)").unsqueeze(2).to_broadcast([P, 8, HD])
                        dve.tensor_tensor(St[:, gs, :], sum_[:, gs, :], decay, ALU.mult).then_inc(s["st"], 1)

                triangles(0, 0)
                substitute(0, 0)
                merged(0, 0)

                def body(n, q):
                    triangles(n + 1, 1 - q)
                    substitute(n + 1, 1 - q)
                    advanced(n, q)
                    merged(n + 1, 1 - q)

                body(0, 0)
                body(1, 1)
                with dve.Fori(1, NCH // 2 - 1) as i:
                    body(2 * i, 0)
                    body(2 * i + 1, 1)
                body(NCH - 2, 0)
                advanced(NCH - 1, 1)


def low_rank_up(nc, sems, name, weight, parts, store):
    with Buffers(nc, name, sems) as b:
        w = [b.sb(f"w{i}", [m, D]) for i, (_f, m, _h, _l) in enumerate(parts)]
        w_hi = [b.sb(f"w_hi{i}", [m, D], F32R) for i, (_f, m, _h, _l) in enumerate(parts)]
        w_lo = [b.sb(f"w_lo{i}", [m, D], F32R) for i, (_f, m, _h, _l) in enumerate(parts)]
        y = b.sb("y", [P, 2, S])
        ps = b.ps("ps", [P, 2, 2, HALF])
        s_w = b.sem("s_w")
        s_hi = b.sem("s_hi")
        s_lo = b.sem("s_lo")
        s_mm = b.sem("s_mm")
        s_y = b.sem("s_y")
        s_st = [b.sem(f"s_st{i}") for i in range(2)]
        with nc.Block() as block:

            @block.sync
            def _(sp):
                for i, (f, m, _h, _l) in enumerate(parts):
                    sp.dma_start(w[i][:, :], weight[f:f + m, :]).then_inc(s_w, 16)
                for n in range(KT):
                    sp.wait_ge(s_y, n + 1)
                    sp.dma_start(store[n * P:(n + 1) * P, :], y[:, n % 2, :]).then_inc(s_st[n % 2], 16)
                for u in range(2):
                    sp.wait_ge(s_st[u], 16 * (KT // 2))

            @block.scalar
            def _(act):
                act.wait_ge(s_w, 16 * len(parts))
                for i in range(len(parts)):
                    act.copy(w_hi[i][:, :], w[i][:, :]).then_inc(s_hi, 1)

            @block.vector
            def _(dve):
                for i in range(len(parts)):
                    dve.wait_ge(s_hi, i + 1)
                    dve.tensor_tensor(w_lo[i][:, :], w[i][:, :], f32(w_hi[i][:, :]), ALU.subtract).then_inc(s_lo, 1)
                for n in range(KT):
                    dve.wait_ge(s_mm, n + 1)
                    after(dve, s_st[n % 2], 16 * (n // 2))
                    dve.tensor_copy(y[:, n % 2, :].rearrange("p (a b) -> p a b", a=2), ps[:, n % 2, :, :]).then_inc(s_y, 1)

            @block.tensor
            def _(pe):
                pe.wait_ge(s_lo, len(parts))
                for n in range(KT):
                    f = slice(n * P, (n + 1) * P)
                    after(pe, s_y, n - 1)
                    for hf in range(2):
                        c = slice(hf * HALF, (hf + 1) * HALF)
                        for i, (_f, m, hi, lo) in enumerate(parts):
                            mm = three_passes(pe, ps[:, n % 2, hf, :], w_hi[i][:, f], w_lo[i][:, f], hi[:, c], lo[:, c],
                                              i == 0, i == len(parts) - 1)
                    mm.then_inc(s_mm, 1)


def finish(nc, sems, io, scr, o_hi, o_lo):
    with Buffers(nc, "fin", sems) as b:
        ya = b.sb("ya", [P, 2, S])
        yb = b.sb("yb", [P, 2, S])
        bo = b.sb("bo", [P, 2, S])
        g = b.sb("g", [P, 2, S])
        d = b.sb("d", [P, 2, S])
        sd = b.sb("sd", [P, 2, S])
        blk = b.sb("blk", [P, P])
        eps = b.sb("eps", [P, 1])
        ln = b.sb("ln", [P, 2, KT])
        pmean = b.ps("pmean", [P, 2, HALF])
        pvar = b.ps("pvar", [P, 2, HALF])
        s_mem = b.sem("s_mem")
        s_ln = b.sem("s_ln")
        s_in = [b.sem(f"s_in{i}") for i in range(2)]
        s_sum = b.sem("s_sum")
        s_mean = b.sem("s_mean")
        s_d = b.sem("s_d")
        s_sq = b.sem("s_sq")
        s_var = b.sem("s_var")
        s_sd = b.sem("s_sd")
        s_r = b.sem("s_r")
        s_y = b.sem("s_y")
        s_hi = b.sem("s_hi")
        s_lo = b.sem("s_lo")

        def two(ap):
            return ap.rearrange("p (a b) -> p a b", a=2)

        with nc.Block() as block:

            @block.sync
            def _(sp):
                sp.dma_start(ln[:, :, :], io["ln"]).then_inc(s_ln, 16)
                for k in range(KT):
                    u = k % 2
                    after(sp, s_lo, k - 1)
                    for dst, j in ((ya, k), (yb, KT + k)):
                        sp.dma_start(dst[:, u, :].rearrange("p (c t) -> p c t", t=CH),
                                     scr["y"][:, :, j, :].rearrange("c p t -> p c t")).then_inc(s_in[u], 16)
                    for dst, src in ((bo, "bonus"), (g, "g")):
                        sp.dma_start(dst[:, u, :], scr[src][k * P:(k + 1) * P, :]).then_inc(s_in[u], 16)

            @block.gpsimd
            def _(pool):
                pool.memset(blk[:, :], 0.0).then_inc(s_mem, 1)
                pool.memset(eps[:, :], GN_EPS).then_inc(s_mem, 1)
                for hh in range(2):
                    pool.wait_ge(s_mem, 2 + hh)
                    pool.memset(blk[HD * hh:HD * hh + HD, HD * hh:HD * hh + HD], 1.0 / HD).then_inc(s_mem, 1)
                pool.wait_ge(s_mem, 4)
                for k in range(KT):
                    pool.wait_ge(s_hi, k + 1)
                    pool.tensor_tensor(o_lo[:, k, :], d[:, k % 2, :], f32(o_hi[:, k, :]), ALU.subtract).then_inc(s_lo, 1)

            @block.scalar
            def _(act):
                act.wait_ge(s_mem, 4)
                for k in range(KT):
                    u = k % 2
                    act.wait_ge(s_d, k + 1)
                    act.activation(sd[:, u, :], d[:, u, :], ACT.Square).then_inc(s_sq, 1)
                    act.wait_ge(s_var, k + 1)
                    act.activation(two(sd[:, u, :]), pvar[:, :, :], ACT.Sqrt, bias=eps[:, :]).then_inc(s_sd, 1)
                    act.wait_ge(s_y, 3 * k + 3)
                    act.copy(o_hi[:, k, :], d[:, u, :]).then_inc(s_hi, 1)

            @block.tensor
            def _(pe):
                pe.wait_ge(s_mem, 4)
                for k in range(KT):
                    u = k % 2
                    pe.wait_ge(s_sum, k + 1)
                    after(pe, s_d, k)
                    for hf in range(2):
                        mm = pe.matmul(pmean[:, hf, :], blk[:, :], ya[:, u, hf * HALF:(hf + 1) * HALF], start=True, stop=True)
                    mm.then_inc(s_mean, 1)
                    pe.wait_ge(s_sq, k + 1)
                    after(pe, s_sd, k)
                    for hf in range(2):
                        mm = pe.matmul(pvar[:, hf, :], blk[:, :], sd[:, u, hf * HALF:(hf + 1) * HALF], start=True, stop=True)
                    mm.then_inc(s_var, 1)

            @block.vector
            def _(dve):
                dve.wait_ge(s_ln, 16)
                for k in range(KT):
                    u = k % 2
                    dve.wait_ge(s_in[u], 64 * (k // 2 + 1))
                    dve.tensor_tensor(ya[:, u, :], ya[:, u, :], yb[:, u, ::-1], ALU.add).then_inc(s_sum, 1)
                    dve.wait_ge(s_sum, k + 1)
                    dve.wait_ge(s_mean, k + 1)
                    after(dve, s_lo, k - 1)
                    dve.tensor_tensor(two(d[:, u, :]), two(ya[:, u, :]), pmean[:, :, :], ALU.subtract).then_inc(s_d, 1)
                    dve.wait_ge(s_sd, k + 1)
                    dve.reciprocal(sd[:, u, :], sd[:, u, :]).then_inc(s_r, 1)
                    dve.wait_ge(s_r, k + 1)
                    dve.wait_ge(s_d, k + 1)
                    dve.scalar_tensor_tensor(d[:, u, :], d[:, u, :], ln[:, 0, k:k + 1], sd[:, u, :], ALU.mult,
                                             ALU.mult).then_inc(s_y, 1)
                    dve.wait_ge(s_y, 3 * k + 1)
                    dve.scalar_tensor_tensor(d[:, u, :], d[:, u, :], ln[:, 1, k:k + 1], bo[:, u, :], ALU.add,
                                             ALU.add).then_inc(s_y, 1)
                    dve.wait_ge(s_y, 3 * k + 2)
                    dve.tensor_tensor(d[:, u, :], d[:, u, :], g[:, u, :], ALU.mult).then_inc(s_y, 1)


def load_tiles(nc, sems, name, dst, src):
    with Buffers(nc, name, sems) as b:
        s_ld = b.sem("s_ld")
        with nc.Block() as block:

            @block.sync
            def _(sp):
                sp.dma_start(dst[:, :, :], src.rearrange("(k p) n -> p k n", p=P)).then_inc(s_ld, 16)
                sp.wait_ge(s_ld, 16)


INPUTS = {
    "x_tok": (S, D), "x_mirror": (FOLD, D), "x_feat": (D, S), "alt": (1, FOLD + 2),
    "cos_tok": (FOLD, FOLD + 2), "sin_tok": (FOLD, FOLD), "cos_grp": (GD, GD), "sin_grp": (GD, GD),
    "fnet_gain": (P, KT), "fnet_w": (D, D), "fnet_b": (P, KT),
    "mix_gain": (P, KT), "ffn_gain": (2, P, KT), "final_gain": (P, KT),
    "mu": (6, P, KT, 2), "w_rkv": (3, D, D), "w1": (D, NZ * RANK), "w2": (NZ * RANK, D),
    "a1": (D, NZ * RANK), "a2": (NZ * RANK, D), "g1": (D, RG), "g2": (RG, D), "vec": (P, 7, KT),
    "ln": (P, 2, KT), "w_o": (D, D), "ffn_in": (2, D, 2 * DFF), "ffn_out": (2, DFF, D), "ffn_conv": (2, P, 2 * FT, 4),
}


def program(nc, io, out, stop=None):
    scr = {n: nc.dram_tensor(f"scr_{n}", list(shape), F32, kind="Internal").ap() for n, shape in {
        "h": (D, S), "hn": (D, S), "r": (D, S), "k": (D, S), "v": (D, S), "g": (D, S), "bonus": (D, S),
        "abrk": (NCH, P, NZ, KT, 4 * CH), "vt": (NZ, S, D), "y": (NCH, P, NZ * KT, CH),
        "blocks": (2, CH // 16, NZ * KT, 16, 16), "inverse": (2, CH // 16, NZ * KT, 16, 16),
        "inverse_t": (2, CH // 16, NZ * KT, 16, 16)}.items()}
    with ExitStack() as sems:

        def act_pair(b, name, shape):
            return b.sb(name + "_hi", shape, F32R), b.sb(name + "_lo", shape, F32R)

        with Buffers(nc, "l0", sems) as top:
            x_hi, x_lo = act_pair(top, "x", [P, KT, S])
            with Buffers(nc, "l0f", sems) as b:
                a = act_pair(b, "a", [P, KT, FOLD + 2])
                bb = act_pair(b, "b", [P, KT, FOLD])
                fnet_tokens(nc, sems, io, x_hi, x_lo, *a, *bb)
                fnet_features(nc, sems, io, *a, *bb, x_hi, x_lo)
            h = top.sb("h", [P, KT, S])
            project(nc, sems, "fo", io["fnet_w"], x_hi, x_lo, h=h, residual=io["x_feat"], bias=io["fnet_b"])
            rms_norm(nc, sems, "n0", h, io["ffn_gain"][0], x_hi, x_lo)
            feed_forward(nc, sems, "f0", h, x_hi, x_lo, io["ffn_in"][0], io["ffn_out"][0], io["ffn_conv"][0])
            rms_norm(nc, sems, "n1", h, io["mix_gain"], store=scr["hn"], save=scr["h"])
        with Buffers(nc, "l1", sems) as top:
            pc = top.sb("pc", [P, NCH, NZ * KT])
            with Buffers(nc, "l1a", sems) as mid:
                hid_w = act_pair(mid, "hw", [P, S])
                hid_a = act_pair(mid, "ha", [P, S])
                with Buffers(nc, "l1b", sems) as b:
                    hn = b.sb("hn", [P, KT, S])
                    x_hi, x_lo = act_pair(b, "x", [P, KT, S])
                    load_tiles(nc, sems, "lh", hn, scr["hn"])
                    for i, n in enumerate("rkv"):
                        token_mix(nc, sems, "m" + n, hn, io["mu"][i], x_hi, x_lo)
                        project(nc, sems, "p" + n, io["w_rkv"][i], x_hi, x_lo, store=scr[n])
                    token_mix(nc, sems, "mw", hn, io["mu"][3], x_hi, x_lo)
                    low_rank_down(nc, sems, "w1", io["w1"], x_hi, x_lo, ACT.Tanh,
                                  [(0, P, hid_w[0][:, :], hid_w[1][:, :])])
                    token_mix(nc, sems, "ma", hn, io["mu"][4], x_hi, x_lo)
                    low_rank_down(nc, sems, "a1", io["a1"], x_hi, x_lo, ACT.Copy,
                                  [(0, P, hid_a[0][:, :], hid_a[1][:, :])])
                    token_mix(nc, sems, "mg", hn, io["mu"][5], x_hi, x_lo)
                    with Buffers(nc, "l1g", sems) as gb:
                        g0 = act_pair(gb, "g0", [P, S])
                        g1 = act_pair(gb, "g1", [RG - P, S])
                        low_rank_down(nc, sems, "g1", io["g1"], x_hi, x_lo, ACT.Sigmoid,
                                      [(0, P, g0[0][:, :], g0[1][:, :]), (P, RG - P, g1[0][:, :], g1[1][:, :])])
                        low_rank_up(nc, sems, "g2", io["g2"], [(0, P, *g0), (P, RG - P, *g1)], scr["g"])
                prepare(nc, sems, io, scr, hid_w, hid_a, pc)
            recurrence(nc, sems, scr, pc)
        with Buffers(nc, "l2", sems) as top:
            x_hi, x_lo = act_pair(top, "x", [P, KT, S])
            h = top.sb("h", [P, KT, S])
            finish(nc, sems, io, scr, x_hi, x_lo)
            project(nc, sems, "ro", io["w_o"], x_hi, x_lo, h=h, residual=scr["h"])
            rms_norm(nc, sems, "n2", h, io["ffn_gain"][1], x_hi, x_lo)
            feed_forward(nc, sems, "f1", h, x_hi, x_lo, io["ffn_in"][1], io["ffn_out"][1], io["ffn_conv"][1])
            rms_norm(nc, sems, "n3", h, io["final_gain"], store=out)


def columns(v):
    return np.ascontiguousarray(np.swapaxes(v.reshape(v.shape[:-1] + (-1, P)), -1, -2))


def tables():
    s = np.arange(FOLD)[:, None]
    c = np.arange(FOLD + 2)[None, :]
    cos = np.cos(2 * np.pi * ((s * c) % S) / S)
    sin = np.sin(2 * np.pi * ((s * c) % S) / S)[:, :FOLD]
    cos[0, :] = 0.5
    cos[:, FOLD + 1] = 0.0
    alt = np.where(np.arange(FOLD + 2) % 2 == 0, 1.0, -1.0)
    alt[FOLD + 1] = 0.0
    k = np.arange(GD)
    ang = 2 * np.pi * ((k[:, None] * k[None, :]) % GD) / GD
    norm = 1.0 / np.sqrt(S * GD)
    return {"cos_tok": cos, "sin_tok": sin, "alt": alt[None, :], "cos_grp": np.cos(ang) * norm,
            "sin_grp": np.sin(ang) * norm}


def layout(x, norm_mix_g, norm_ffn_g, norm_final_g, fnet_w_o, fnet_b_o, rwkv_mu, rwkv_w_rkv, rwkv_w0, rwkv_w1,
           rwkv_w2, rwkv_a0, rwkv_a1, rwkv_a2, rwkv_g1, rwkv_g2, rwkv_k_k, rwkv_k_a, rwkv_r_k, rwkv_ln_w, rwkv_ln_b,
           rwkv_w_o, ffn_w_in, ffn_conv_w, ffn_conv_b, ffn_w_out):
    tok = x[0]
    mirror = tok[(S - np.arange(FOLD)) % S]
    mu = np.moveaxis(columns(rwkv_mu[0]), 0, -1)
    vec = np.stack([columns(v) for v in (rwkv_k_k[0], rwkv_k_a[0], rwkv_r_k[0].reshape(-1), rwkv_w0[0, 0],
                                         rwkv_w0[0, 1], rwkv_a0[0, 0], rwkv_a0[0, 1])], axis=1)
    taps = np.concatenate([ffn_conv_w, ffn_conv_b[:, None, :]], axis=1)
    conv = np.stack([np.moveaxis(columns(taps[i]), 0, -1) for i in range(2)])
    down = lambda w: np.moveaxis(w[0], 0, 1).reshape(D, -1)
    up = lambda w: w[0].reshape(-1, D)
    return {
        "x_tok": tok, "x_mirror": mirror, "x_feat": tok.T,
        "fnet_gain": columns(norm_mix_g[0]), "fnet_w": fnet_w_o[0], "fnet_b": columns(fnet_b_o[0]),
        "mix_gain": columns(norm_mix_g[1]), "ffn_gain": columns(norm_ffn_g), "final_gain": columns(norm_final_g),
        "mu": mu, "w_rkv": rwkv_w_rkv[0], "w1": down(rwkv_w1), "w2": up(rwkv_w2), "a1": down(rwkv_a1),
        "a2": up(rwkv_a2), "g1": rwkv_g1[0], "g2": rwkv_g2[0], "vec": vec,
        "ln": np.stack([columns(rwkv_ln_w[0]), columns(rwkv_ln_b[0])], axis=1), "w_o": rwkv_w_o[0],
        "ffn_in": ffn_w_in, "ffn_out": ffn_w_out, "ffn_conv": conv,
    }


def kernel(**inputs):
    from concourse import bacc
    from concourse.bass_utils import run_bass_kernel_spmd

    arrays = layout(**{k: np.asarray(v) for k, v in inputs.items()})
    arrays.update({k: v.astype(np.float32) for k, v in tables().items()})
    arrays = {k: np.ascontiguousarray(arrays[k]) for k in INPUTS}
    nc = bacc.Bacc("TRN2", target_bir_lowering=False, num_devices=1)
    io = {}
    for name, shape in INPUTS.items():
        assert arrays[name].shape == shape, (name, arrays[name].shape, shape)
        io[name] = nc.dram_tensor(name, list(shape), F32, kind="ExternalInput").ap()
    out = nc.dram_tensor("out", [D, S], F32, kind="ExternalOutput").ap()
    program(nc, io, out)
    r = run_bass_kernel_spmd(nc, [arrays], core_ids=[0])
    return np.ascontiguousarray(r.results[0]["out"].T)[None]
```
